# Optimizing a Trainium2 kernel written in Bass

```python
import jax
import jax.numpy as jnp
from jax import lax
import numpy as np

D_MODEL = 1024
BATCH = 1
SEQ = 512
DEPTH = 2

CTX_LEN = 256
GRID_W = 64
ROPE_THETA = 10000.0
RMS_EPS = 1e-6
QBLK = 128
NEG_INF = -1e30
N_BRANCH = 3

MLA_HEADS = 8
MLA_NOPE = 64
MLA_ROPE = 32
MLA_V = 64
MLA_Q_RANK = 384
MLA_KV_RANK = 256
MLA_WIDTH = MLA_HEADS * MLA_V
MLA_SCALE = (MLA_NOPE + MLA_ROPE) ** -0.5

SWA_HEADS = 8
SWA_KV_HEADS = 2
SWA_GROUP = SWA_HEADS // SWA_KV_HEADS
SWA_HEAD_DIM = 64
SWA_WIDTH = SWA_HEADS * SWA_HEAD_DIM
SWA_KV_WIDTH = SWA_KV_HEADS * SWA_HEAD_DIM
WINDOW = 128
SWA_BAND = QBLK + 2 * WINDOW
SWA_SCALE = SWA_HEAD_DIM ** -0.5

AX_HEADS = 8
AX_KV_HEADS = 2
AX_GROUP = AX_HEADS // AX_KV_HEADS
AX_HEAD_DIM = 64
AX_WIDTH = AX_HEADS * AX_HEAD_DIM
AX_KV_WIDTH = AX_KV_HEADS * AX_HEAD_DIM
AX_SCALE = AX_HEAD_DIM ** -0.5

KV_SPLITS = (MLA_KV_RANK, MLA_ROPE, SWA_KV_WIDTH, SWA_KV_WIDTH, AX_KV_WIDTH, AX_KV_WIDTH)
Q_SPLITS = (MLA_Q_RANK, SWA_WIDTH, AX_WIDTH, MLA_WIDTH, SWA_WIDTH, AX_WIDTH, N_BRANCH * D_MODEL)
KV_COLS = sum(KV_SPLITS)
IN_WIDTH = KV_COLS + sum(Q_SPLITS)

kernel_name = 'hybrid_mla_swa_axial_parallel_dit_block'

def _split(t, sizes):
    offs = np.cumsum(sizes)[:-1].tolist()
    return jnp.split(t, offs, axis=-1)

def rmsnorm(x, w):
    xf = x.astype(jnp.float32)
    y = xf * lax.rsqrt(jnp.mean(xf * xf, axis=-1, keepdims=True) + RMS_EPS)
    return (y * w.astype(jnp.float32)).astype(x.dtype)

def rope_1d(x, pos):
    d = x.shape[-1]
    T = x.shape[1]
    freqs = ROPE_THETA ** (-jnp.arange(0, d, 2, dtype=jnp.float32) / d)
    ang = pos.astype(jnp.float32)[:, None] * freqs[None, :]
    bshape = (T,) + (1,) * (x.ndim - 3) + (d // 2,)
    cos = jnp.cos(ang).reshape(bshape)
    sin = jnp.sin(ang).reshape(bshape)
    xf = x.astype(jnp.float32)
    x1, x2 = xf[..., : d // 2], xf[..., d // 2:]
    return jnp.concatenate([x1 * cos - x2 * sin, x1 * sin + x2 * cos], axis=-1).astype(x.dtype)

def rope_axial(x, pos_row, pos_col):
    h = x.shape[-1] // 2
    return jnp.concatenate([rope_1d(x[..., :h], pos_row), rope_1d(x[..., h:], pos_col)], axis=-1)

def _rope_fn(pos):
    if pos is None:
        return lambda t: t
    return lambda t: rope_axial(t, pos[0], pos[1])

def attend(q, k, v, scale, mask=None, sink=None):
    s = jnp.einsum('bqhgd,bkhd->bhgqk', q.astype(jnp.float32), k.astype(jnp.float32)) * scale
    if mask is not None:
        s = jnp.where(mask, s, NEG_INF)
    if sink is not None:
        sk = jnp.broadcast_to(sink.astype(jnp.float32)[None, :, :, None, None], s.shape[:-1] + (1,))
        p = jax.nn.softmax(jnp.concatenate([s, sk], axis=-1), axis=-1)[..., :-1]
    else:
        p = jax.nn.softmax(s, axis=-1)
    o = jnp.einsum('bhgqk,bkhd->bqhgd', p, v.astype(jnp.float32))
    return o.astype(v.dtype)

def dense_latent_attention(q, k, v, k_ctx, v_ctx, scale):
    B, T, Hkv, G, Dk = q.shape
    nb = T // QBLK
    kk = jnp.concatenate([k_ctx, k], axis=1)
    vv = jnp.concatenate([v_ctx, v], axis=1)
    qb = jnp.moveaxis(q.reshape(B, nb, QBLK, Hkv, G, Dk), 1, 0)
    ob = lax.map(lambda qi: attend(qi, kk, vv, scale), qb)
    return jnp.moveaxis(ob, 0, 1).reshape(B, T, Hkv, G, -1)

def window_latent_attention(q, k, v, k_ctx, v_ctx, sink, scale):
    B, T, Hkv, G, Dk = q.shape
    nb = T // QBLK
    Lc = k_ctx.shape[1]
    pad = ((0, 0), (WINDOW, WINDOW), (0, 0), (0, 0))
    kp = jnp.pad(k, pad)
    vp = jnp.pad(v, pad)
    qb = jnp.moveaxis(q.reshape(B, nb, QBLK, Hkv, G, Dk), 1, 0)
    k_off = jnp.arange(SWA_BAND, dtype=jnp.int32) - WINDOW
    rel = k_off[None, :] - jnp.arange(QBLK, dtype=jnp.int32)[:, None]
    local = jnp.abs(rel) <= WINDOW
    ctx_mask = jnp.ones((QBLK, Lc), dtype=bool)

    def block(args):
        i, qi = args
        start = i * QBLK
        kb = lax.dynamic_slice_in_dim(kp, start, SWA_BAND, axis=1)
        vb = lax.dynamic_slice_in_dim(vp, start, SWA_BAND, axis=1)
        k_abs = start + k_off
        valid = (k_abs >= 0) & (k_abs < T)
        mask = jnp.concatenate([ctx_mask, local & valid[None, :]], axis=1)
        kk = jnp.concatenate([k_ctx, kb], axis=1)
        vv = jnp.concatenate([v_ctx, vb], axis=1)
        return attend(qi, kk, vv, scale, mask=mask, sink=sink)

    ob = lax.map(block, (jnp.arange(nb, dtype=jnp.int32), qb))
    return jnp.moveaxis(ob, 0, 1).reshape(B, T, Hkv, G, -1)

def project_kv(p, lw, pos):
    B, T, _ = p.shape
    rope = _rope_fn(pos)
    ckv, kr, sk, sv, ak, av = _split(p, KV_SPLITS)
    kv_m = (rmsnorm(ckv, lw['mla_kv_norm']) @ lw['mla_w_ukv']).reshape(B, T, MLA_HEADS, MLA_NOPE + MLA_V)
    k_rope = rope(kr.reshape(B, T, 1, MLA_ROPE))
    k_m = jnp.concatenate([kv_m[..., :MLA_NOPE], jnp.broadcast_to(k_rope, (B, T, MLA_HEADS, MLA_ROPE))], axis=-1)
    v_m = kv_m[..., MLA_NOPE:]
    k_s = rope(sk.reshape(B, T, SWA_KV_HEADS, SWA_HEAD_DIM))
    v_s = sv.reshape(B, T, SWA_KV_HEADS, SWA_HEAD_DIM)
    k_a = rope(rmsnorm(ak.reshape(B, T, AX_KV_HEADS, AX_HEAD_DIM), lw['ax_k_norm']))
    v_a = av.reshape(B, T, AX_KV_HEADS, AX_HEAD_DIM)
    return k_m, v_m, k_s, v_s, k_a, v_a

def project_q(p, lw, pos):
    B, T, _ = p.shape
    rope = _rope_fn(pos)
    cq, sq, aq, z_m, z_s, z_a, g = _split(p, Q_SPLITS)
    q_m = (rmsnorm(cq, lw['mla_q_norm']) @ lw['mla_w_uq']).reshape(B, T, MLA_HEADS, 1, MLA_NOPE + MLA_ROPE)
    q_m = jnp.concatenate([q_m[..., :MLA_NOPE], rope(q_m[..., MLA_NOPE:])], axis=-1)
    q_s = rope(sq.reshape(B, T, SWA_KV_HEADS, SWA_GROUP, SWA_HEAD_DIM))
    q_a = rope(rmsnorm(aq.reshape(B, T, AX_KV_HEADS, AX_GROUP, AX_HEAD_DIM), lw['ax_q_norm']))
    return q_m, q_s, q_a, z_m, z_s, z_a, g

def merge_branches(o_m, o_s, o_a, z_m, z_s, z_a, g, lw):
    B, T = o_m.shape[:2]
    y_m = (o_m.reshape(B, T, MLA_WIDTH) * jax.nn.silu(z_m)) @ lw['w_o_mla']
    y_s = (o_s.reshape(B, T, SWA_WIDTH) * jax.nn.silu(z_s)) @ lw['w_o_swa']
    y_a = (o_a.reshape(B, T, AX_WIDTH) * jax.nn.silu(z_a)) @ lw['w_o_ax']
    g_m, g_s, g_a = jnp.split(g, N_BRANCH, axis=-1)
    y = jax.nn.sigmoid(g_m) * y_m + jax.nn.sigmoid(g_s) * y_s + jax.nn.sigmoid(g_a) * y_a
    return y @ lw['w_out']

def hybrid_layer(x, ctx, c, c_ctx, lw, pos, update_ctx):
    mod_x = jax.nn.silu(c) @ lw['ada_w'] + lw['ada_b']
    mod_c = jax.nn.silu(c_ctx) @ lw['ada_w'] + lw['ada_b']
    shift, scale, gate = jnp.split(mod_x[:, None, :], 3, axis=-1)
    c_shift, c_scale, c_gate = jnp.split(mod_c, 3, axis=-1)
    h = rmsnorm(x, lw['norm_w']) * (1 + scale) + shift
    hc = rmsnorm(ctx, lw['norm_w']) * (1 + c_scale) + c_shift

    p = h @ lw['w_in']
    k_m, v_m, k_s, v_s, k_a, v_a = project_kv(p[..., :KV_COLS], lw, pos)
    q_m, q_s, q_a, z_m, z_s, z_a, g = project_q(p[..., KV_COLS:], lw, pos)
    kc_m, vc_m, kc_s, vc_s, kc_a, vc_a = project_kv(hc @ lw['w_in'][:, :KV_COLS], lw, None)

    sink = lw['swa_sink'].reshape(SWA_KV_HEADS, SWA_GROUP)
    o_m = dense_latent_attention(q_m, k_m, v_m, kc_m, vc_m, MLA_SCALE)
    o_s = window_latent_attention(q_s, k_s, v_s, kc_s, vc_s, sink, SWA_SCALE)
    o_a = dense_latent_attention(q_a, k_a, v_a, kc_a, vc_a, AX_SCALE)
    x = x + gate * merge_branches(o_m, o_s, o_a, z_m, z_s, z_a, g, lw)

    if update_ctx:
        qc_m, qc_s, qc_a, zc_m, zc_s, zc_a, gc = project_q(hc @ lw['w_in'][:, KV_COLS:], lw, None)
        oc_m = attend(qc_m, kc_m, vc_m, MLA_SCALE)
        oc_s = attend(qc_s, kc_s, vc_s, SWA_SCALE, sink=sink)
        oc_a = attend(qc_a, kc_a, vc_a, AX_SCALE)
        ctx = ctx + c_gate * merge_branches(oc_m, oc_s, oc_a, zc_m, zc_s, zc_a, gc, lw)
    return x, ctx

def setup_inputs(seed: int = 0) -> dict:
    key = jax.random.key(seed)
    ks = jax.random.split(key, 20)
    D = D_MODEL
    f32 = jnp.float32

    def nrm(k, shape, scale):
        return jax.random.normal(k, shape, f32) * scale

    return {
        'x': nrm(ks[0], (BATCH, SEQ, D), 1.0),
        'c': nrm(ks[1], (BATCH, D), 1.0),
        'ctx': nrm(ks[2], (BATCH, CTX_LEN, D), 1.0),
        'c_ctx': nrm(ks[3], (D,), 1.0),
        'ada_w': nrm(ks[4], (DEPTH, D, 3 * D), 0.5 * D ** -0.5),
        'ada_b': nrm(ks[5], (DEPTH, 3 * D), 0.02),
        'norm_w': 1.0 + nrm(ks[6], (DEPTH, D), 0.1),
        'w_in': nrm(ks[7], (DEPTH, D, IN_WIDTH), D ** -0.5),
        'mla_q_norm': 1.0 + nrm(ks[8], (DEPTH, MLA_Q_RANK), 0.1),
        'mla_w_uq': nrm(ks[9], (DEPTH, MLA_Q_RANK, MLA_HEADS * (MLA_NOPE + MLA_ROPE)), MLA_Q_RANK ** -0.5),
        'mla_kv_norm': 1.0 + nrm(ks[10], (DEPTH, MLA_KV_RANK), 0.1),
        'mla_w_ukv': nrm(ks[11], (DEPTH, MLA_KV_RANK, MLA_HEADS * (MLA_NOPE + MLA_V)), MLA_KV_RANK ** -0.5),
        'swa_sink': nrm(ks[12], (DEPTH, SWA_HEADS), 0.5),
        'ax_q_norm': 1.0 + nrm(ks[13], (DEPTH, AX_HEAD_DIM), 0.1),
        'ax_k_norm': 1.0 + nrm(ks[14], (DEPTH, AX_HEAD_DIM), 0.1),
        'w_o_mla': nrm(ks[15], (DEPTH, MLA_WIDTH, D), MLA_WIDTH ** -0.5),
        'w_o_swa': nrm(ks[16], (DEPTH, SWA_WIDTH, D), SWA_WIDTH ** -0.5),
        'w_o_ax': nrm(ks[17], (DEPTH, AX_WIDTH, D), AX_WIDTH ** -0.5),
        'w_out': nrm(ks[18], (DEPTH, D, D), D ** -0.5),
        'final_norm_w': 1.0 + nrm(ks[19], (D,), 0.1),
    }

def reference(x, c, ctx, c_ctx, ada_w, ada_b, norm_w, w_in, mla_q_norm, mla_w_uq, mla_kv_norm, mla_w_ukv,
              swa_sink, ax_q_norm, ax_k_norm, w_o_mla, w_o_swa, w_o_ax, w_out, final_norm_w):
    T = x.shape[1]
    rows = T // GRID_W
    pos_row = jnp.repeat(jnp.arange(rows, dtype=jnp.int32), GRID_W)
    pos_col = jnp.tile(jnp.arange(GRID_W, dtype=jnp.int32), rows)
    pos = (pos_row, pos_col)
    for l in range(DEPTH):
        lw = {
            'ada_w': ada_w[l], 'ada_b': ada_b[l], 'norm_w': norm_w[l], 'w_in': w_in[l],
            'mla_q_norm': mla_q_norm[l], 'mla_w_uq': mla_w_uq[l],
            'mla_kv_norm': mla_kv_norm[l], 'mla_w_ukv': mla_w_ukv[l],
            'swa_sink': swa_sink[l], 'ax_q_norm': ax_q_norm[l], 'ax_k_norm': ax_k_norm[l],
            'w_o_mla': w_o_mla[l], 'w_o_swa': w_o_swa[l], 'w_o_ax': w_o_ax[l], 'w_out': w_out[l],
        }
        x, ctx = hybrid_layer(x, ctx, c, c_ctx, lw, pos, update_ctx=(l < DEPTH - 1))
    return rmsnorm(x, final_norm_w)


_drawn_inputs = setup_inputs


def setup_inputs(seed=0):
    import zlib

    import numpy as np

    out = dict(_drawn_inputs(seed))
    spreads = {}
    factors = {'ctx': 4.329,
     'ada_b': 7.68,
     'norm_w': 6.974,
     'mla_q_norm': 8.0,
     'mla_w_uq': 4.461,
     'mla_kv_norm': 8.0,
     'swa_sink': 8.0,
     'ax_q_norm': 8.0,
     'ax_k_norm': 8.0}
    for name, (base, spread) in spreads.items():
        noise = np.random.default_rng([zlib.crc32(name.encode()), seed]).standard_normal(out[name].shape)
        drawn = base * np.exp(spread * noise) if base else spread * noise
        out[name] = jnp.asarray(drawn.astype(out[name].dtype))
    for name, factor in factors.items():
        out[name] = (out[name] * factor).astype(out[name].dtype)
    return out
```

```python
import concourse.bass as bass
from concourse import mybir
from contextlib import ExitStack

D = 1024
CTX, SEQ = 256, 512
TOK = CTX + SEQ
LAYERS = 2
P = 128
KD = D // P
TT_CTX, TT = CTX // P, TOK // P
HEADS, KVH, HD = 8, 2, 64
MLA_NOPE, MLA_ROPE, MLA_V = 64, 32, 64
MLA_K = MLA_NOPE + MLA_ROPE
Q_RANK, KV_RANK = 384, 256
KQ, KKV = Q_RANK // P, KV_RANK // P
WIDTH = HEADS * HD
KO = WIDTH // P
WINDOW = 128
EPS = 1e-6
NEG = -1e30
GRID_W, THETA = 64, 10000.0
C_CKV, C_KR = 0, 256
C_SK, C_SV, C_AK, C_AV = 288, 416, 544, 672
C_CQ = 800
C_Q = {"swa": 1184, "ax": 1696}
C_Z = {"mla": 2208, "swa": 2720, "ax": 3232}
C_G = {"mla": 3744, "swa": 4768, "ax": 5792}
BRANCHES = ("mla", "swa", "ax")
SCALE = {"mla": float(MLA_K) ** -0.5, "swa": float(HD) ** -0.5, "ax": float(HD) ** -0.5}

V_C, V_CC = 0, KD
V_L = 2 * KD
V_NORM, V_QN, V_KVN, V_AXQ, V_AXK = 0, KD, KD + KQ, KD + KQ + KKV, KD + KQ + KKV + 1
V_PER = KD + KQ + KKV + 2
V_ROWS = V_L + LAYERS * V_PER

K_ID, K_ONE, K_BLK, K_MPREV, K_MNEXT, K_SEL, K_END = 0, 128, 256, 384, 512, 640, 642

CHUNK = 1024
RAW_SLOTS, SPLIT_SLOTS = 3, 4


def tokens(group):
    return (0, CTX) if group == "c" else (CTX, SEQ)
E_UNITS = 5


def token_groups(l):
    return ("x", "c") if l + 1 < LAYERS else ("x",)


def token_tiles(l):
    return list(range(TT)) if l + 1 < LAYERS else list(range(TT_CTX, TT))


def passes(l, branch):
    out = []
    for h in range(HEADS):
        for tg in token_groups(l):
            units = []
            for tt in (range(TT_CTX, TT) if tg == "x" else range(TT_CTX)):
                masks, lo = [], 0
                if branch != "swa":
                    pieces = [(0, 0, 512), (512, 512, TOK - 512)] if tg == "x" else [(0, 0, CTX)]
                    width = TOK if tg == "x" else CTX
                    kts = {k: k * P for k in range(width // P)}
                else:
                    lo, pieces, kts = 254, [(256, 0, CTX)], {0: 2, 1: 2 + P}
                    width = 2 + CTX
                    if tg == "x":
                        q = tt - TT_CTX
                        k0, k1 = max(q - 1, 0), min(q + 2, SEQ // P)
                        pieces.append((512, CTX + k0 * P, (k1 - k0) * P))
                        masks = [(512 + (k - k0) * P, 0 if k < q else 1) for k in range(k0, k1) if k != q]
                        kts.update({TT_CTX + k: 2 + CTX + (k - k0) * P for k in range(k0, k1)})
                        width += (k1 - k0) * P
                units.append(dict(l=l, branch=branch, h=h, tt=tt, pieces=pieces, masks=masks, kts=kts, lo=lo, width=width))
            out.append(dict(l=l, branch=branch, h=h, tg=tg, units=units))
    return out


def schedule():
    events, chunks, later = [], [], []
    n = dict(acc=0, ev_a=0, free=0, rope=0, stat=0, h=0, l=0, th=0, s=0, pt=0, o=0, x=0, f=0, xr=0, mod=0,
             split=0, tab=0, axt=0, ada=0, xl=0)
    bank_last = {0: None, 1: None}
    chunk_last, th_last = {}, {0: None, 1: None}
    turn = [0]

    def emit(ev, **e):
        events.append(dict(ev=ev, **e))

    def tick():
        for item in list(later):
            item[0] -= 1
            if item[0] <= 0:
                later.remove(item)
                item[1]()

    def flush():
        while later:
            later.pop(0)[1]()

    def bank():
        turn[0] ^= 1
        return turn[0]

    def chunk(kind, *where):
        chunks.append((kind,) + where)
        return len(chunks) - 1

    def group(kind, bank_no, parts=1, chunk_ids=(), oldest=None, hl=False, needs=None, act=True, dve=True, **kw):
        g = dict(kind=kind, bank=bank_no, chunks=list(chunk_ids), parts=parts, act=act, dve=dve, hl=hl, **kw)

        def step(part):
            def run():
                if part == 0:
                    g.update(n=n["acc"], before=bank_last[bank_no], passes=n["o"], needs=needs() if needs else {})
                    n["acc"] += 1
                    bank_last[bank_no] = g
                    if chunk_ids:
                        while n["split"] < (chunk_ids[0] if oldest is None else oldest) + SPLIT_SLOTS:
                            c = n["split"]
                            emit("W", c=c, reuse=chunk_last.get(c - SPLIT_SLOTS, 0))
                            n["split"] += 1
                    for c in chunk_ids:
                        chunk_last[c] = g["n"] + 1
                emit("G", g=g, part=part)
                if part == parts - 1:
                    read_out()
                tick()
            return run

        def read_out():
            if g.get("roped"):
                flush()
                g["rope_prev"] = (n["rope"], n["l"])
                n["rope"] += 1
                g["rope"], g["tab"], g["axt"] = n["rope"], n["tab"], n["axt"]
            if act:
                n["ev_a"] += 1
                g["a"] = n["ev_a"]
            if dve:
                n["free"] += 1
                g["v"] = n["free"]
            if kind == "statb":
                n["stat"] += 1
                g["stat"] = n["stat"]
            if kind in ("z", "g"):
                g["th_slot"] = 0 if g["tg"] == "x" else 1
                g["th_before"] = th_last[g["th_slot"]]
            if kind == "z" or (kind == "y" and g["branch"] != BRANCHES[0]):
                n["th"] += 1
                g["th"] = n["th"]
            if kind == "z":
                th_last[g["th_slot"]] = g
            if kind == "y":
                th_last[g["of"]["th_slot"]] = g
            if kind == "wout":
                n["xr"] += 1
                g["xr"] = n["xr"]
            if kind == "ada":
                n["ada"] += 1
            emit("E", g=g)
            if hl:
                later.append([1, high])

        def high():
            n["h"] += 1
            g["high_n"] = n["h"]
            emit("H", g=g)
            later.append([1, low])

        def low():
            n["l"] += 1
            g["low_n"] = n["l"]
            emit("L", g=g)

        g["steps"] = [step(p) for p in range(parts)]
        return g

    def go(g):
        for s in g["steps"]:
            s()
        return g

    def weave(main, fill):
        done = 0
        for i, s in enumerate(main):
            s()
            while done < (i + 1) * len(fill) // len(main):
                fill[done]()
                done += 1

    def project(kind, l, c, tg, bank_no, parts=1, src="h", co=0, m=P, width=P, k=KD, needs=None, **kw):
        need = needs or (lambda x=n["x"]: dict(x_l=x))
        return group(kind, bank_no, parts, (c,), l=l, mode="w", src=src, co=co, m=m, width=width, k=k, tg=tg, needs=need, **kw)

    def roped(tg, squares=False):
        return dict(roped=True, hl=True, act=squares) if tg == "x" else dict(roped=False)

    def load_table(which):
        flush()
        emit("TAB", which=which, free=n["free"], rope=n["rope"])
        n["tab"] += 1

    def attention(l, branch, fills, ready, ready_v):
        ps = passes(l, branch)
        owner = {}

        def S(u):
            if any(g["hl"] and "low_n" not in g for g in ready[u["h"]]):
                flush()
            u.update(n=n["s"], slot=n["s"] % E_UNITS, x=n["x"],
                     ready_free=max(g["v"] for g in ready[u["h"]]), ready_l=max(g.get("low_n", 0) for g in ready[u["h"]]))
            n["s"] += 1
            emit("S", u=u)

        def M(u):
            before = owner.get(u["slot"])
            assert before is None or before["done"]
            u["e_free"] = before["pt_end"] if before else 0
            owner[u["slot"]] = u["pa"]
            emit("M", u=u)

        def slot_free(u):
            before = owner.get(u["slot"])
            return before is None or before["done"]

        for pa in ps:
            pa["done"] = False
            for u in pa["units"]:
                u["pa"] = pa
        us = ps[0]["units"]
        for k, u in enumerate(us):
            S(u)
            M(u)
            if k:
                emit("N", u=us[k - 1])
        emit("N", u=us[-1])
        for i, pa in enumerate(ps):
            us = ps[i + 1]["units"] if i + 1 < len(ps) else []
            kts = sorted({k for u in pa["units"] for k in u["kts"]})
            tiles = []
            for j, kt in enumerate(kts):
                q = [i for i, u in enumerate(pa["units"]) if kt in u["kts"]]
                tiles.append(dict(n=n["pt"] + j, kt=kt, q0=q[0], q1=q[-1] + 1, pa=pa, first=j == 0, last=j == len(kts) - 1))
            n["pt"] += len(tiles)
            pa.update(pt_end=n["pt"], o=n["o"], tiles=tiles)
            n["o"] += 1
            queue = list(us)
            wait_m, wait_n = [], []
            main = []

            def advance():
                if wait_m and slot_free(wait_m[0]):
                    u = wait_m.pop(0)
                    M(u)
                    wait_n.append(u)
                    if len(wait_n) > 1:
                        emit("N", u=wait_n.pop(0))
                if queue and len(wait_m) < 2:
                    u = queue.pop(0)
                    S(u)
                    wait_m.append(u)
                tick()

            def tile_step(j):
                def run():
                    if j == 0:
                        pa["bank1"] = bank_last[1]
                    emit("T", t=tiles[j])
                    if j:
                        emit("PV", t=tiles[j - 1])
                    if j == len(tiles) - 1:
                        pa["done"] = True
                    tick()
                    advance()
                return run

            def last_value():
                assert all("v" in g for g in ready_v[pa["h"] // 2])
                emit("PV", t=tiles[-1])
                advance()

            def out():
                emit("O", pa=pa)

            def rest():
                advance()

            main = [tile_step(j) for j in range(len(tiles))] + [last_value] + [rest] * len(us) + [out]
            for t in tiles:
                t["ready_v"] = ready_v[pa["h"] // 2]
            weave(main, fills(i, ps))
            while queue or wait_m:
                advance()
            while wait_n:
                emit("N", u=wait_n.pop(0))

    def ada(l, js, after):
        for j in js:
            slot = n["ada"] % 2
            cc = (chunk("ada", l, j, 0, slot, ada_reader[slot]), chunk("ada", l, j, 1))
            go(group("ada", bank(), chunk_ids=cc, act=False, mode="ada", l=l, j=j, slot=slot, needs=lambda: dict(cs_ready=1)))
            after(j, slot)

    def ada_columns(l):
        def columns(j, slot):
            go(group("adaT", bank(), act=False, mode="adaT", l=l, j=j, slot=slot, needs=lambda: dict(acc_free=n["free"], loads=(n["ada"] + 1) // 2)))
            ada_reader[slot] = n["acc"]
        ada(l, range(2 * D // 256), columns)
        emit("MOD", l=l, free=n["free"])
        n["mod"] += 1

    def ada_gates(l):
        def rows(j, slot):
            for s in range(len(token_groups(l))):
                go(group("adaG", bank(), act=False, mode="adaG", l=l, j=j, s=s, slot=slot, needs=lambda: dict(acc_free=n["free"], loads=(n["ada"] + 1) // 2)))
            ada_reader[slot] = n["acc"]
        ada(l, range(2 * D // 256, 3 * D // 256), rows)

    ada_reader = {0: 0, 1: 0}

    def z_and_merge(l, b):
        branch = BRANCHES[b]
        for t in range(KO):
            c = chunk("win", l, C_Z[branch] + t * P, P)
            for tg in token_groups(l):
                go(project("z", l, c, tg, bank(), branch=branch, t=t, hl=True, o_done=n["o"]))
        flush()
        og = n["l"]
        for t in range(KD):
            cg, cy = chunk("win", l, C_G[branch] + t * P, P), chunk("wo", l, b, t)
            gates = {tg: go(project("g", l, cg, tg, bank(), branch=branch, t=t, dve=False)) for tg in token_groups(l)}
            for tg in token_groups(l):
                go(project("y", l, cy, tg, bank(), src="og", k=KO, branch=branch, t=t, of=gates[tg], hl=(b == 2), act=False,
                           needs=lambda og=og: dict(l_done=og)))
        flush()

    for l in range(LAYERS):
        tgs, tts = token_groups(l), token_tiles(l)
        if l == 0:
            emit("XL", l=0, tail=False, acc=0, l_done=0, h=0, rope=0)
            n["xl"] += 1
            ada_columns(0)
        for tt in range(TT):
            emit("XN", l=l, tt=tt, n=n["x"], s=n["s"], xr=n["xr"], mod=n["mod"], acc=n["acc"], xl=n["xl"])
            n["x"] += 1

        load_table("m")
        cks = [chunk("win", l, C_CKV + t * P, P) for t in range(KKV)]
        for t in range(KKV):
            for tg in ("x", "c"):
                go(project("ckv", l, cks[t], tg, bank(), t=t))
        c = chunk("win", l, C_KR, MLA_ROPE)
        for tg in ("x", "c"):
            go(project("kr", l, c, tg, bank(), m=MLA_ROPE, width=MLA_ROPE, what="kr", **roped(tg)))
        for tg in ("x", "c"):
            go(group("statb", bank(), mode="statb", l=l, tg=tg, what="ckv", hl=True, tiles=KKV, nsum=KV_RANK, needs=lambda: dict(ev_a=n["ev_a"])))
        for t in range(KQ):
            c = chunk("win", l, C_CQ + t * P, P)
            for tg in tgs:
                go(project("cq", l, c, tg, bank(), what="cq", t=t))
        flush()
        go(group("statq", bank(), mode="statq", l=l, what="mla", tts=tts, tiles=KQ, needs=lambda: dict(ev_a=n["ev_a"])))
        latents = dict(acc_free=n["free"], l_done=n["l"])
        ready, ready_v, steps = {}, {}, {}

        def mla_pair(p, bank_of, parts):
            cq, ck = chunk("uq", l, p), chunk("ukv", l, p)
            for h in (2 * p, 2 * p + 1):
                gs = [project("qm", l, cq, tg, bank_of(), parts, src="cq", co=(h % 2) * MLA_K, m=MLA_K, width=2 * MLA_K, k=KQ,
                              needs=lambda: latents, what="qm", head=h, **roped(tg)) for tg in tgs]
                ready[h] = gs
                steps[h] = [s for g in gs for s in g["steps"]]
            for h in (2 * p, 2 * p + 1):
                gs = [project("km", l, ck, tg, bank_of(), parts, src="ckv", oldest=cq, co=(h % 2) * P, m=MLA_NOPE, width=2 * P, k=KKV,
                              needs=lambda: latents, what="km", head=h) for tg in ("x", "c")]
                ready[h] = ready[h] + gs
                steps[h] += [s for g in gs for s in g["steps"]]
            ready_v[p] = [group("vm", bank_of(), chunk_ids=(ck,), oldest=cq, mode="vm", l=l, tt=tt, what="vm", pair=p, needs=lambda: latents) for tt in range(TT)]
            steps[2 * p] += [s for g in ready_v[p] for s in g["steps"]]

        mla_pair(0, bank, 1)
        for h in (0, 1):
            for s in steps[h]:
                s()
        flush()
        ahead = 1 if len(tgs) == 2 else 2

        def mla_fill(i, ps):
            h = ps[i]["h"] + ahead
            if ps[i]["tg"] != "x" or h < 2 or h >= HEADS:
                return []
            if h % 2 == 0:
                mla_pair(h // 2, lambda: 0, 2)
            return steps[h]

        attention(l, "mla", mla_fill, ready, ready_v)
        flush()
        ada_reader.update({0: n["acc"], 1: n["acc"]})
        z_and_merge(l, 0)

        load_table("s")
        c = chunk("win", l, C_SK, P)
        keys = [go(project("ks", l, c, tg, bank(), what="k", **roped(tg))) for tg in ("x", "c")]
        cc = (chunk("v", l, 0), chunk("v", l, 1))
        values = [go(group("vs", bank(), chunk_ids=cc, mode="vs", l=l, tt=tt, what="vs", needs=lambda: dict(x_l=n["x"]))) for tt in range(TT)]
        flush()
        for branch in ("swa", "ax"):
            if branch == "ax":
                load_table("s")
                emit("AXT", l=l, which=V_AXK, tab=n["tab"])
                n["axt"] += 1
                c = chunk("win", l, C_AK, P)
                for tg in ("x", "c"):
                    go(project("ak", l, c, tg, bank(), roped=(tg == "x")))
                keys = [go(group("statb", bank(), mode="statb", l=l, tg=tg, what="ak", hl=True, tiles=1, nsum=HD,
                                 needs=lambda: dict(ev_a=n["ev_a"]), rope_done=n["rope"])) for tg in ("x", "c")]
                load_table("s")
                emit("AXT", l=l, which=V_AXQ, tab=n["tab"])
                n["axt"] += 1
            ready, ready_v = {}, {p: values for p in range(HEADS // 2)}

            def q_pair(t, bank_of, parts):
                c = chunk("win", l, C_Q[branch] + t * P, P)
                gs = [project("qs", l, c, tg, bank_of(), parts, what="qs", head=2 * t, branch=branch,
                              **roped(tg, squares=branch == "ax")) for tg in tgs]
                if branch == "ax":
                    gs.append(group("statq", bank_of(), mode="statq", l=l, what="ax", head=2 * t, tts=tts, tiles=1, needs=lambda: dict(ev_a=n["ev_a"])))
                for h in (2 * t, 2 * t + 1):
                    ready[h] = gs + keys
                return [s for g in gs for s in g["steps"]]

            for s in q_pair(0, bank, 1):
                s()
            flush()

            def q_fill(i, ps):
                h = ps[i]["h"]
                if h % 2 or ps[i]["tg"] != "x" or h + 2 >= HEADS:
                    return []
                return q_pair(h // 2 + 1, lambda: 0, 3)

            attention(l, branch, q_fill, ready, ready_v)
            flush()
            z_and_merge(l, BRANCHES.index(branch))

        y_ready = n["l"]
        emit("XL", l=l, tail=True, acc=n["acc"], l_done=n["l"], h=n["h"], rope=n["rope"])
        n["xl"] += 1
        ada_gates(l)
        gates = n["free"]
        if l + 1 < LAYERS:
            ada_columns(l + 1)
        for j in range(D // 256):
            cc = (chunk("wout", l, j, 0), chunk("wout", l, j, 1))
            for tt in tts:
                go(group("wout", bank(), chunk_ids=cc, act=False, mode="wout", l=l, j=j, tt=tt, xl=n["xl"],
                         gates=gates, needs=lambda: dict(l_done=y_ready)))
        if l + 1 < LAYERS:
            emit("XS", l=l, xr=n["xr"])
        else:
            for tt in tts:
                emit("FN", tt=tt, n=n["f"], xr=n["xr"])
                n["f"] += 1
    return events, chunks


def build(nc, t_in, out):
    F, R = mybir.dt.float32, mybir.dt.float32r
    ALU, ACT, AX = mybir.AluOpType, mybir.ActivationFunctionType, mybir.AxisListType
    events, chunks = schedule()
    x_mid = nc.dram_tensor("x_mid", [SEQ, D], F, kind="Internal").ap()

    base = [(nc.sbuf_base + 31) // 32 * 32]

    def fixed(name, shape, dt):
        size = 4
        for s in shape[1:]:
            size *= s
        t = nc.alloc_sbuf_tensor_at(name, shape, dt, offset=base[0])
        base[0] += (size + 31) // 32 * 32
        return t

    h_hi, h_lo = fixed("h_hi", [P, KD, TOK], R), fixed("h_lo", [P, KD, TOK], R)
    w_raw = fixed("w_raw", [P, RAW_SLOTS, CHUNK], F)
    w_hi, w_lo = fixed("w_hi", [P, SPLIT_SLOTS, CHUNK], R), fixed("w_lo", [P, SPLIT_SLOTS, CHUNK], R)
    cos, sin = fixed("cos", [P, SEQ], F), fixed("sin", [P, SEQ], F)
    swapped, rot = fixed("swapped", [P, SEQ], F), fixed("rot", [P, SEQ], F)
    o_half = fixed("o_half", [P, SEQ], F)
    ident, ones, blk = fixed("ident", [P, P], F), fixed("ones", [P, P], F), fixed("blk", [P, P], F)
    ident_r, mask_r = fixed("ident_r", [P, P], R), fixed("mask_r", [P, 2, P], R)
    sel = fixed("sel", [5, 2], F)
    vec, vec_sw = fixed("vec", [P, V_ROWS], F), fixed("vec_sw", [P, V_ROWS], F)
    cs = fixed("cs", [P, KD, 4], R)
    cs_f = fixed("cs_f", [P, 2, 2 * KD], F)
    mod_col, mod_a = fixed("mod_col", [P, 2 * KD, 2], F), fixed("mod_a", [P, 2, KD], F)
    rq = fixed("rq", [P, HEADS, TT], F)
    nmax, nbias, esum, einv = (fixed(k, [P, 8], F) for k in ("nmax", "nbias", "esum", "einv"))
    ssq, rstd = fixed("ssq", [P, TT], F), fixed("rstd", [P, TT], F)
    sink_in, sink = fixed("sink_in", [1, LAYERS * HEADS], F), fixed("sink", [1, LAYERS * HEADS, 2], F)
    eps_col = fixed("eps_col", [P, 3], F)
    start = base[0]
    ends = []

    def shared(name, shape, dt, at):
        size = 4
        for s in shape[1:]:
            size *= s
        ends.append(start + at + size)
        return nc.alloc_sbuf_tensor_at(name, shape, dt, offset=start + at)

    FEAT = TOK * 4
    y2, y_lo = shared("y2", [P, KD, TOK], F, 0), shared("y_lo", [P, KD, TOK], R, 0)
    o_t = shared("o_t", [P, KO, TOK], F, 24576)
    og_hi, og_lo = shared("og_hi", [P, KO, TOK], R, 36864), shared("og_lo", [P, KO, TOK], R, 49152)
    th = shared("th", [P, 2, SEQ], F, 61440)
    y_hi = shared("y_hi", [P, KD, TOK], R, 65536)
    q_m = shared("q_m", [P, 2, 2, TOK], R, 36864)
    q_s = shared("q_s", [P, 4, TOK], R, 36864)
    e_m = shared("e_m", [P, E_UNITS, TOK], F, 49152)
    pt_m = shared("pt_m", [P, 2, 2, SEQ], R, 49152 + E_UNITS * FEAT)
    k_m = shared("k_m", [P, 2, 2, TOK], R, 72704)
    v_m = shared("v_m", [P, 2, TT, 2, 2, HD], R, 84992)
    cq_hi, cq_lo = shared("cq_hi", [P, KQ, TOK], R, 0), shared("cq_lo", [P, KQ, TOK], R, KQ * FEAT)
    ckv_hi, ckv_lo = shared("ckv_hi", [P, KKV, TOK], R, 18432), shared("ckv_lo", [P, KKV, TOK], R, 97280)
    e_s = shared("e_s", [P, E_UNITS, 896], F, 49152)
    pt_s = shared("pt_s", [P, 2, 2, SEQ], R, 67072)
    k_s = shared("k_s", [P, KVH, 2, TOK], R, 75264)
    v_s = shared("v_s", [P, TT, 2 * KVH, 2, HD], R, 87552)
    lat_f, lat_sq = shared("lat_f", [P, KKV, TOK], F, 49152), shared("lat_sq", [P, KKV, TOK], F, 55296)
    lat_r = shared("lat_r", [P, TOK], F, 61440)
    cq_sq = shared("cq_sq", [P, KQ, TOK], F, 24576)
    aq_sq_x, aq_sq_c = shared("aq_sq_x", [P, SEQ], F, 72704), shared("aq_sq_c", [P, CTX], F, 99840)
    xres = shared("xres", [P, TT, D], F, 24576)
    gate = shared("gate", [P, 2, D], F, 49152)
    x_add = shared("x_add", [P, 256], F, 57344)
    a_row = shared("a_row", [5, 2, 256], F, 101792)
    xn = shared("xn", [P, 2, D], F, 90112)
    x_mod = shared("x_mod", [P, D], F, 60416)
    fin_w = shared("fin_w", [P, D], F, 60416)
    v_rows = shared("v_rows", [V_ROWS, P], F, 60416)
    mask_f = shared("mask_f", [P, 2 * P], F, 61440)
    x_rows = t_in["x"][0, :, :].rearrange("(t p) d -> p t d", p=P)
    out_rows = out[0, :, :].rearrange("(t p) d -> p t d", p=P)

    small_loads = {
        "const_load": [(ident[:, :], t_in["consts"][:, K_ID:K_ID + P]), (ones[:, :], t_in["consts"][:, K_ONE:K_ONE + P]),
                       (blk[:, :], t_in["consts"][:, K_BLK:K_BLK + P]), (mask_f[:, :], t_in["consts"][:, K_MPREV:K_MPREV + 2 * P]),
                       (sel[:, :], t_in["consts"][0:5, K_SEL:K_SEL + 2])],
        "vec_load": [(v_rows[V_C:V_C + KD, :], t_in["c"][0, :].rearrange("(k p) -> k p", p=P)),
                     (v_rows[V_CC:V_CC + KD, :], t_in["c_ctx"].rearrange("(k p) -> k p", p=P)),
                     (sink_in[:, :], t_in["swa_sink"].rearrange("l h -> (l h)").rearrange("(a n) -> a n", a=1))],
    }
    for l in range(LAYERS):
        r = V_L + l * V_PER
        small_loads["vec_load"] += [
            (v_rows[r + V_NORM:r + V_NORM + KD, :], t_in["norm_w"][l, :].rearrange("(k p) -> k p", p=P)),
            (v_rows[r + V_QN:r + V_QN + KQ, :], t_in["mla_q_norm"][l, :].rearrange("(k p) -> k p", p=P)),
            (v_rows[r + V_KVN:r + V_KVN + KKV, :], t_in["mla_kv_norm"][l, :].rearrange("(k p) -> k p", p=P))]
        for v, name in ((V_AXQ, "ax_q_norm"), (V_AXK, "ax_k_norm")):
            for half in range(2):
                small_loads["vec_load"].append((v_rows[r + v:r + v + 1, half * HD:(half + 1) * HD], t_in[name][l:l + 1, :]))
    CONST_LOADS, VEC_LOADS = len(small_loads["const_load"]), len(small_loads["vec_load"])
    X_LOADS = [4, 5]
    assert max(ends) <= nc.sbuf_usable_end, (max(ends), nc.sbuf_usable_end)

    with ExitStack() as stack:
        def psum(name, cols):
            return stack.enter_context(nc.psum_tensor(name, [P, cols], F))

        acc = [psum("acc0", 512), psum("acc1", 512)]
        wide = [psum("wide0", 1024), psum("wide1", 1024)]
        ptp = [psum("ptp0", 512), psum("ptp1", 512)]

        def semaphore(name):
            return stack.enter_context(nc.semaphore(name))

        const_load, vec_load, tab_load, fin_load = (semaphore(k) for k in ("const_load", "vec_load", "tab_load", "fin_load"))
        x_load, x_saved = semaphore("x_load"), semaphore("x_saved")
        raw_load = [semaphore(f"raw_load{i}") for i in range(RAW_SLOTS)]
        bias_load, out_saved = ([semaphore(f"{k}{i}") for i in range(2)] for k in ("bias_load", "out_saved"))
        vec_done, vec_ready, consts_ready = semaphore("vec_done"), semaphore("vec_ready"), semaphore("consts_ready")
        cs_th, cs_ready, mod_ready = semaphore("cs_th"), semaphore("cs_ready"), semaphore("mod_ready")
        w_hi_ready, w_lo_ready = semaphore("w_hi_ready"), semaphore("w_lo_ready")
        acc_done, ev_a, acc_free = semaphore("acc_done"), semaphore("ev_a"), semaphore("acc_free")
        h_done, l_done = semaphore("h_done"), semaphore("l_done")
        rope_link, rope_done, axt_ready = semaphore("rope_link"), semaphore("rope_done"), semaphore("axt_ready")
        stat_done, th_done = semaphore("stat_done"), semaphore("th_done")
        s_done, max_done, exp_done, norm_done = (semaphore(k) for k in ("s_done", "max_done", "exp_done", "norm_done"))
        pt_done, pt_hi_ready, pt_lo_ready = semaphore("pt_done"), semaphore("pt_hi_ready"), semaphore("pt_lo_ready")
        pv_done, o_copied, o_free = semaphore("pv_done"), semaphore("o_copied"), semaphore("o_free")
        x_sq, x_stat, x_n, x_t = (semaphore(k) for k in ("x_sq", "x_stat", "x_n", "x_t"))
        x_f, x_b, x_h, x_l = (semaphore(k) for k in ("x_f", "x_b", "x_h", "x_l"))
        xr_done, f_ready, chain_v = semaphore("xr_done"), semaphore("f_ready"), semaphore("chain_v")
        block = stack.enter_context(nc.Block())

        def counting():
            seen = {}

            def new(semaphore_, count):
                higher = count > seen.get(id(semaphore_), 0)
                if higher:
                    seen[id(semaphore_)] = count
                return higher
            return new

        def cols(tg):
            return slice(0, CTX) if tg == "c" else slice(CTX, TOK)

        def size(tg):
            return CTX if tg == "c" else SEQ

        def f(ap):
            return ap.bitcast(F)

        def chunk_dma(c):
            kind, l = chunks[c][0], chunks[c][1]
            raw = w_raw[:, c % RAW_SLOTS, :]
            if kind == "win":
                c0, w = chunks[c][2:]
                return [(raw[:, 0:KD * w].rearrange("p (k c) -> p k c", k=KD),
                         t_in["w_in"][l, :, c0:c0 + w].rearrange("(k p) c -> p k c", p=P))]
            if kind == "v":
                half = chunks[c][2]
                rows = slice(half * D // 2, (half + 1) * D // 2)
                dst = raw.rearrange("p (k c) -> p k c", k=KD // 2)
                return [(dst[:, :, i * P:(i + 1) * P], t_in["w_in"][l, rows, c0:c0 + P].rearrange("(k p) c -> p k c", p=P))
                        for i, c0 in enumerate((C_SV, C_AV))]
            if kind in ("ada", "wout"):
                j, half = chunks[c][2:4]
                src = t_in["ada_w" if kind == "ada" else "w_out"]
                return [(raw.rearrange("p (k c) -> p k c", k=KD // 2),
                         src[l, half * D // 2:(half + 1) * D // 2, j * 256:(j + 1) * 256].rearrange("(k p) c -> p k c", p=P))]
            if kind == "uq":
                w, p = 2 * MLA_K, chunks[c][2]
                return [(raw[:, 0:KQ * w].rearrange("p (k c) -> p k c", k=KQ),
                         t_in["mla_w_uq"][l, :, p * w:(p + 1) * w].rearrange("(k p) c -> p k c", p=P))]
            if kind == "ukv":
                w, p = 2 * P, chunks[c][2]
                return [(raw[:, 0:KKV * w].rearrange("p (k c) -> p k c", k=KKV),
                         t_in["mla_w_ukv"][l, :, p * w:(p + 1) * w].rearrange("(k p) c -> p k c", p=P))]
            b, t = chunks[c][2:]
            src = t_in[("w_o_mla", "w_o_swa", "w_o_ax")[b]]
            return [(raw[:, 0:KO * P].rearrange("p (k c) -> p k c", k=KO),
                     src[l, :, t * P:(t + 1) * P].rearrange("(k p) c -> p k c", p=P))]

        def chunk_size(c):
            return {"win": KD * (chunks[c][3] if chunks[c][0] == "win" else 0), "v": CHUNK, "ada": CHUNK, "wout": CHUNK,
                    "uq": KQ * 2 * MLA_K, "ukv": KKV * 2 * P, "wo": KO * P}[chunks[c][0]]

        loads = [0] * len(chunks)
        for c in range(len(chunks)):
            loads[c] = (loads[c - RAW_SLOTS] if c >= RAW_SLOTS else 0) + 16 * len(chunk_dma(c))

        @block.sync
        def _(sp):
            new = counting()
            for c in range(len(chunks)):
                if c >= RAW_SLOTS:
                    if new(w_lo_ready, c - RAW_SLOTS + 1):
                        sp.wait_ge(w_lo_ready, c - RAW_SLOTS + 1)
                for dst, src in chunk_dma(c):
                    sp.dma_start(dst, src).then_inc(raw_load[c % RAW_SLOTS], 16)
                if chunks[c][0] == "ada" and chunks[c][3] == 0:
                    l, j, _, slot, reader = chunks[c][1:]
                    if reader:
                        if new(acc_done, reader):
                            sp.wait_ge(acc_done, reader)
                    sp.dma_start(a_row[4:5, slot, :], t_in["ada_b"][l:l + 1, j * 256:(j + 1) * 256]).then_inc(bias_load[slot], 16)

        def q_of(u):
            cs_ = slice(u["tt"] * P, (u["tt"] + 1) * P)
            if u["branch"] == "mla":
                return [q_m[0:MLA_K, u["h"] % 2, i, cs_] for i in range(2)]
            return [q_s[:, u["h"] % 4, cs_]]

        def k_of(u, k0, nk):
            if u["branch"] == "mla":
                return [k_m[0:MLA_K, u["h"] % 2, i, k0:k0 + nk] for i in range(2)]
            return [k_s[:, u["h"] // (HEADS // KVH), i, k0:k0 + nk] for i in range(2)]

        def v_of(pa, kt):
            if pa["branch"] == "mla":
                v = v_m[:, (pa["h"] // 2) % 2, kt, pa["h"] % 2, :, :]
            else:
                v = v_s[:, kt, (KVH if pa["branch"] == "ax" else 0) + pa["h"] // (HEADS // KVH), :, :]
            return v.rearrange("p a d -> p (a d)")

        def e_of(u, c0=0, c1=None):
            e = e_m if u["branch"] != "swa" else e_s
            return e[:, u["slot"], c0:(u["width"] if c1 is None else c1)]

        def pt_of(t, part):
            p = pt_m if t["pa"]["branch"] != "swa" else pt_s
            return p[:, t["n"] % 2, part, t["q0"] * P:t["q1"] * P]

        def o_rows(pa):
            return (slice(0, HD), slice(HD, P)) if pa["h"] % 2 == 0 else (slice(HD, P), slice(0, HD))

        def matmuls(g):
            a = acc[g["bank"]]
            out_ = []

            def run(dst, pairs):
                for i, (lhs, rhs) in enumerate(pairs):
                    out_.append((dst, lhs, rhs, i == 0, i == len(pairs) - 1))

            def split3(lh, ll, rh, rl):
                return [(lh, rh), (lh, rl), (ll, rh)]

            mode = g["mode"]
            if mode == "w":
                s = g["chunks"][0] % SPLIT_SLOTS
                hi, lo = {"h": (h_hi, h_lo), "cq": (cq_hi, cq_lo), "ckv": (ckv_hi, ckv_lo), "og": (og_hi, og_lo)}[g["src"]]
                pairs = []
                for k in range(g["k"]):
                    c0 = k * g["width"] + g["co"]
                    w = slice(c0, c0 + g["m"])
                    pairs += [(w_hi[:, s, w], hi[:, k, cols(g["tg"])]), (w_hi[:, s, w], lo[:, k, cols(g["tg"])]),
                              (w_lo[:, s, w], hi[:, k, cols(g["tg"])])]
                run(a[0:g["m"], 0:size(g["tg"])], pairs)
            elif mode in ("vs", "wout", "ada"):
                hi, lo = (h_hi, h_lo) if mode == "vs" else (y_hi, y_lo)
                pairs = []
                for k in range(KD):
                    s = g["chunks"][k // (KD // 2)] % SPLIT_SLOTS
                    w = slice((k % (KD // 2)) * 256, (k % (KD // 2) + 1) * 256)
                    if mode == "ada":
                        pairs += [(cs[:, k, :], w_hi[:, s, w]), (cs[:, k, :], w_lo[:, s, w])]
                    else:
                        ts = slice(g["tt"] * P, (g["tt"] + 1) * P)
                        pairs += split3(hi[:, k, ts], lo[:, k, ts], w_hi[:, s, w], w_lo[:, s, w])
                run(a[0:4 if mode == "ada" else P, 0:256], pairs)
            elif mode == "vm":
                s = g["chunks"][0] % SPLIT_SLOTS
                pairs = []
                for k in range(KKV):
                    wv = [w[:, s, k * 256:(k + 1) * 256].rearrange("p (h a d) -> p h a d", h=2, a=2)[:, :, 1, :] for w in (w_hi, w_lo)]
                    ts = slice(g["tt"] * P, (g["tt"] + 1) * P)
                    pairs += split3(ckv_hi[:, k, ts], ckv_lo[:, k, ts], *wv)
                run(a[:, 0:2 * HD], pairs)
            elif mode == "statb":
                m = ones if g["what"] == "ckv" else blk
                run(a[:, 0:size(g["tg"])], [(m[:, :], lat_sq[:, t, cols(g["tg"])]) for t in range(g["tiles"])])
            elif mode == "statq":
                for tt in g["tts"]:
                    ts = slice(tt * P, (tt + 1) * P)
                    if g["what"] == "mla":
                        run(a[:, 2 * tt:2 * tt + 2], [(cq_sq[:, t, ts], ones[:, 0:2]) for t in range(KQ)])
                    else:
                        sq = aq_sq_c[:, ts] if tt < TT_CTX else aq_sq_x[:, (tt - TT_CTX) * P:(tt - TT_CTX + 1) * P]
                        run(a[:, 2 * tt:2 * tt + 2], [(sq, blk[:, 0:P:HD])])
            elif mode == "adaT":
                for i in range(2):
                    run(a[:, 2 * i:2 * i + 2], [(a_row[0:5, g["slot"], i * P:(i + 1) * P], sel[0:5, :])])
            elif mode == "adaG":
                run(a[:, 0:256], [(sel[0:5, g["s"]:g["s"] + 1].to_broadcast([5, P]), a_row[0:5, g["slot"], :])])
            return out_

        @block.tensor
        def _(pe):
            new = counting()
            if new(const_load, 16 * CONST_LOADS):
                pe.wait_ge(const_load, 16 * CONST_LOADS)
            if new(vec_load, 16 * VEC_LOADS):
                pe.wait_ge(vec_load, 16 * VEC_LOADS)
            nc.tensor.transpose(acc[0][:, 0:V_ROWS], v_rows[:, :], ident[0:V_ROWS, 0:V_ROWS]).then_inc(vec_done, 1)
            if new(vec_ready, 1):
                pe.wait_ge(vec_ready, 1)
            if new(consts_ready, 1):
                pe.wait_ge(consts_ready, 1)
            for e in events:
                ev = e["ev"]
                if ev == "G":
                    g, part, mode = e["g"], e["part"], e["g"]["mode"]
                    if part == 0:
                        need = g["needs"]
                        if mode == "vs" or (mode == "w" and g["src"] == "h"):
                            if new(x_l, need["x_l"]):
                                pe.wait_ge(x_l, need["x_l"])
                        elif mode == "vm" or (mode == "w" and g["src"] != "og"):
                            if new(acc_free, need["acc_free"]):
                                pe.wait_ge(acc_free, need["acc_free"])
                            if new(l_done, need["l_done"]):
                                pe.wait_ge(l_done, need["l_done"])
                        elif mode in ("w", "wout"):
                            if new(l_done, need["l_done"]):
                                pe.wait_ge(l_done, need["l_done"])
                        elif mode in ("statb", "statq"):
                            if new(ev_a, need["ev_a"]):
                                pe.wait_ge(ev_a, need["ev_a"])
                        elif mode == "ada":
                            if new(cs_ready, 1):
                                pe.wait_ge(cs_ready, 1)
                        else:
                            if new(acc_free, need["acc_free"]):
                                pe.wait_ge(acc_free, need["acc_free"])
                            if new(bias_load[g["slot"]], 16 * need["loads"]):
                                pe.wait_ge(bias_load[g["slot"]], 16 * need["loads"])
                        if g["chunks"]:
                            if new(w_lo_ready, g["chunks"][-1] + 1):
                                pe.wait_ge(w_lo_ready, g["chunks"][-1] + 1)
                        before = g["before"]
                        if before is not None and before["dve"]:
                            if new(acc_free, before["v"]):
                                pe.wait_ge(acc_free, before["v"])
                        elif before is not None:
                            if new(ev_a, before["a"]):
                                pe.wait_ge(ev_a, before["a"])
                        if g["bank"] == 1:
                            if new(o_free, g["passes"]):
                                pe.wait_ge(o_free, g["passes"])
                    mm = matmuls(g)
                    a, b = part * len(mm) // g["parts"], (part + 1) * len(mm) // g["parts"]
                    for dst, lhs, rhs, first, last in mm[a:b]:
                        ins = nc.tensor.matmul(dst, lhs, rhs, start=first, stop=last)
                    if part == g["parts"] - 1:
                        ins.then_inc(acc_done, 1)
                elif ev == "S":
                    u = e["u"]
                    if new(acc_free, u["ready_free"]):
                        pe.wait_ge(acc_free, u["ready_free"])
                    if new(l_done, u["ready_l"]):
                        pe.wait_ge(l_done, u["ready_l"])
                    if u["n"] >= 2:
                        if new(exp_done, u["n"] - 1):
                            pe.wait_ge(exp_done, u["n"] - 1)
                    if new(x_f, u["x"]):
                        pe.wait_ge(x_f, u["x"])
                    w = wide[u["n"] % 2]
                    if u["branch"] == "swa":
                        i = u["l"] * HEADS + u["h"]
                        nc.tensor.matmul(w[:, u["lo"]:u["lo"] + 2], ones[0:1, :], sink[0:1, i, :], start=True, stop=True)
                    for c0, k0, nk in u["pieces"]:
                        qs, ks = q_of(u), k_of(u, k0, nk)
                        pairs = [(qs[0], ks[0]), (qs[0], ks[1])] + ([(qs[1], ks[0])] if len(qs) == 2 else [])
                        masks = [m for m in u["masks"] if c0 <= m[0] < c0 + nk]
                        for i, (lhs, rhs) in enumerate(pairs):
                            ins = nc.tensor.matmul(w[:, c0:c0 + nk], lhs, rhs, start=(i == 0), stop=(i == len(pairs) - 1 and not masks))
                        for i, (m0, which) in enumerate(masks):
                            ins = nc.tensor.matmul(w[:, m0:m0 + P], ident_r[:, :], mask_r[:, which, :], start=False, stop=(i == len(masks) - 1))
                    ins.then_inc(s_done, 1)
                elif ev == "T":
                    t = e["t"]
                    us = t["pa"]["units"][t["q0"]:t["q1"]]
                    if new(norm_done, us[-1]["n"] + 1):
                        pe.wait_ge(norm_done, us[-1]["n"] + 1)
                    if t["n"] >= 2:
                        if new(pt_lo_ready, t["n"] - 1):
                            pe.wait_ge(pt_lo_ready, t["n"] - 1)
                    for i, u in enumerate(us):
                        c0 = u["kts"][t["kt"]]
                        ins = nc.tensor.transpose(ptp[t["n"] % 2][:, (t["q0"] + i) * P:(t["q0"] + i + 1) * P], e_of(u, c0, c0 + P), ident[:, :])
                    ins.then_inc(pt_done, 1)
                elif ev == "PV":
                    t, pa = e["t"], e["t"]["pa"]
                    if new(pt_lo_ready, t["n"] + 1):
                        pe.wait_ge(pt_lo_ready, t["n"] + 1)
                    if new(acc_free, max(g["v"] for g in t["ready_v"])):
                        pe.wait_ge(acc_free, max(g["v"] for g in t["ready_v"]))
                    if t["first"]:
                        if new(o_free, pa["o"]):
                            pe.wait_ge(o_free, pa["o"])
                        before = pa["bank1"]
                        if before is not None and before["dve"]:
                            if new(acc_free, before["v"]):
                                pe.wait_ge(acc_free, before["v"])
                        elif before is not None:
                            if new(ev_a, before["a"]):
                                pe.wait_ge(ev_a, before["a"])
                    dst = acc[1][:, t["q0"] * P:t["q1"] * P]
                    nc.tensor.matmul(dst, v_of(pa, t["kt"]), pt_of(t, 0), start=t["first"], stop=False)
                    nc.tensor.matmul(dst, v_of(pa, t["kt"]), pt_of(t, 1), start=False, stop=t["last"]).then_inc(pv_done, 1)
                elif ev == "XN":
                    tt, i = e["tt"], e["n"]
                    if new(x_n, i + 1):
                        pe.wait_ge(x_n, i + 1)
                    if new(exp_done, e["s"]):
                        pe.wait_ge(exp_done, e["s"])
                    if i >= 2:
                        if new(x_f, i - 1):
                            pe.wait_ge(x_f, i - 1)
                    for k in range(KD):
                        ins = nc.tensor.transpose(wide[i % 2][:, k * P:(k + 1) * P], xn[:, i % 2, k * P:(k + 1) * P], ident[:, :])
                    ins.then_inc(x_t, 1)

        def pieces(g):
            tg, what, l = g.get("tg"), g["what"], g["l"]
            c = cols(tg) if tg else None
            v0 = V_L + l * V_PER
            src = acc[g["bank"]]
            N = size(tg) if tg else None
            if g.get("roped"):
                src = rot
            if what == "cq":
                return [(cq_hi[:, g["t"], c], cq_lo[:, g["t"], c], src[:, 0:N])], vec[:, v0 + V_QN + g["t"]:v0 + V_QN + g["t"] + 1]
            if what == "qm":
                s = g["head"] % 2
                return [(q_m[0:MLA_K, s, 0, c], q_m[0:MLA_K, s, 1, c], src[0:MLA_K, 0:N])], None
            if what == "km":
                s = g["head"] % 2
                return [(k_m[0:MLA_NOPE, s, 0, c], k_m[0:MLA_NOPE, s, 1, c], src[0:MLA_NOPE, 0:N])], None
            if what == "kr":
                rows = slice(MLA_NOPE, MLA_K)
                s = src[rows, 0:N] if g["roped"] else src[0:MLA_ROPE, 0:N]
                return [(k_m[rows, i, 0, c], k_m[rows, i, 1, c], s) for i in range(2)], None
            if what in ("k", "ak"):
                if what == "ak":
                    src, N0 = lat_f[:, 0, :], c
                else:
                    N0 = slice(0, N)
                out_ = []
                for kv in range(KVH):
                    rows = slice(kv * HD, (kv + 1) * HD)
                    for half in range(2):
                        d = slice(half * HD, (half + 1) * HD)
                        out_.append((k_s[d, kv, 0, c], k_s[d, kv, 1, c], src[rows, N0], k_s[rows, kv, 0, c]))
                return out_, None
            if what == "ckv":
                return [(ckv_hi[:, :, c], ckv_lo[:, :, c], lat_f[:, :, c])], None
            if what == "qs":
                s = g["head"] % 4
                up, dn = slice(0, HD), slice(HD, P)
                w = None
                if g["branch"] == "ax" and not g["roped"]:
                    w = vec[:, v0 + V_AXQ:v0 + V_AXQ + 1]
                return [(q_s[up, s, c], q_s[dn, s, c], src[up, 0:N]), (q_s[dn, s + 1, c], q_s[up, s + 1, c], src[dn, 0:N])], w
            if what == "vs":
                return [(v_s[:, g["tt"], :, 0, :], v_s[:, g["tt"], :, 1, :], src[:, 0:256].rearrange("p (g d) -> p g d", d=HD))], None
            if what == "vm":
                s = g["pair"] % 2
                return [(v_m[:, s, g["tt"], :, 0, :], v_m[:, s, g["tt"], :, 1, :], src[:, 0:2 * HD].rearrange("p (g d) -> p g d", d=HD))], None
            raise KeyError(what)

        def rows_of(ap, w):
            s = ap.start_partition if not callable(ap.start_partition) else ap.start_partition()
            return w[s:s + ap.shape[0], :]

        def high_parts(ps, w):
            for p in ps:
                if w is None:
                    ins = nc.scalar.activation(p[0], p[2], ACT.Copy)
                else:
                    ins = nc.scalar.activation(p[0], p[2], ACT.Identity, scale=rows_of(p[2], w))
            return ins

        def low_parts(ps, w):
            for p in ps:
                hi = p[3] if len(p) == 4 else p[0]
                if w is None:
                    ins = nc.vector.tensor_tensor(p[1], p[2], f(hi), ALU.subtract)
                else:
                    ins = nc.vector.scalar_tensor_tensor(p[1], p[2], rows_of(p[2], w), f(hi), ALU.mult, ALU.subtract)
            return ins

        DIRECT = ("cq", "qm", "km", "kr", "ks", "qs", "vs", "vm")

        def squares_of(g):
            c = cols(g["tg"]) if "tg" in g else None
            if g["kind"] == "cq":
                return cq_sq[:, g["t"], c]
            if g["kind"] in ("ckv", "ak"):
                return lat_sq[:, g.get("t", 0), c]
            if g["kind"] == "qs" and g["branch"] == "ax":
                return (aq_sq_c if g["tg"] == "c" else aq_sq_x)[:, :]
            return None

        @block.scalar
        def _(act):
            new = counting()
            for dst, src in small_loads["const_load"]:
                act.dma_start(dst, src).then_inc(const_load, 16)
            for dst, src in small_loads["vec_load"]:
                act.dma_start(dst, src).then_inc(vec_load, 16)
            if new(const_load, 16 * CONST_LOADS):
                act.wait_ge(const_load, 16 * CONST_LOADS)
            nc.scalar.activation(ident_r[:, :], ident[:, :], ACT.Copy)
            nc.scalar.activation(mask_r[:, :, :], mask_f[:, :].rearrange("p (a b) -> p a b", a=2), ACT.Copy).then_inc(consts_ready, 1)
            if new(vec_ready, 1):
                act.wait_ge(vec_ready, 1)
            nc.scalar.activation(cs_f[:, 0, :], vec[:, 0:2 * KD], ACT.Tanh, scale=0.5).then_inc(cs_th, 1)
            tabs = xl = 0
            for e in events:
                ev = e["ev"]
                if ev == "W" and e["c"] < len(chunks):
                    c = e["c"]
                    if new(raw_load[c % RAW_SLOTS], loads[c]):
                        act.wait_ge(raw_load[c % RAW_SLOTS], loads[c])
                    if new(acc_done, e["reuse"]):
                        act.wait_ge(acc_done, e["reuse"])
                    k = chunk_size(c)
                    nc.scalar.activation(w_hi[:, c % SPLIT_SLOTS, 0:k], w_raw[:, c % RAW_SLOTS, 0:k], ACT.Copy).then_inc(w_hi_ready, 1)
                elif ev == "E" and e["g"]["act"]:
                    g = e["g"]
                    kind, src = g["kind"], acc[g["bank"]]
                    N = size(g["tg"]) if "tg" in g else None
                    if new(acc_done, g["n"] + 1):
                        act.wait_ge(acc_done, g["n"] + 1)
                    sq = squares_of(g)
                    ins = None
                    if sq is not None:
                        ins = nc.scalar.activation(sq, src[:, 0:N], ACT.Square)
                    if kind in DIRECT and not g.get("roped"):
                        ins = high_parts(*pieces(g))
                    elif kind == "statb":
                        if new(stat_done, g["stat"] - 1):
                            act.wait_ge(stat_done, g["stat"] - 1)
                        ins = nc.scalar.activation(lat_r[:, cols(g["tg"])], src[:, 0:N], ACT.Sqrt, scale=1.0 / g["nsum"], bias=eps_col[:, 0:1])
                    elif kind == "statq":
                        t0, t1 = g["tts"][0], g["tts"][-1] + 1
                        got = src[:, 2 * t0:2 * t1].rearrange("p (t a) -> p a t", a=2)
                        if g["what"] == "mla":
                            dst, got, count, col = rq[:, 0, t0:t1], got[:, 0, :], Q_RANK, 1
                        else:
                            dst, count, col = rq[:, g["head"]:g["head"] + 2, t0:t1], HD, 2
                        s2 = SCALE[g["what"]] ** 2
                        ins = nc.scalar.activation(dst, got, ACT.Sqrt, scale=1.0 / (count * s2), bias=eps_col[:, col:col + 1])
                    elif kind in ("z", "g"):
                        before = g["th_before"]
                        if before is not None and "th" in before:
                            if new(th_done, before["th"]):
                                act.wait_ge(th_done, before["th"])
                        elif before is not None:
                            if new(acc_free, before["v"]):
                                act.wait_ge(acc_free, before["v"])
                        ins = nc.scalar.activation(th[:, g["th_slot"], 0:N], src[:, 0:N], ACT.Tanh, scale=0.5)
                    ins.then_inc(ev_a, 1)
                elif ev == "H":
                    g = e["g"]
                    if g["kind"] == "statb":
                        if new(stat_done, g["stat"]):
                            act.wait_ge(stat_done, g["stat"])
                        ins = high_parts(*pieces(g))
                    elif g["kind"] == "z":
                        if new(th_done, g["th"]):
                            act.wait_ge(th_done, g["th"])
                        ins = nc.scalar.activation(og_hi[:, g["t"], cols(g["tg"])], o_t[:, g["t"], cols(g["tg"])], ACT.Copy)
                    elif g["kind"] == "y":
                        if new(th_done, g["th"]):
                            act.wait_ge(th_done, g["th"])
                        ins = nc.scalar.activation(y_hi[:, g["t"], cols(g["tg"])], y2[:, g["t"], cols(g["tg"])], ACT.Copy, scale=0.5)
                    else:
                        if new(rope_done, g["rope"]):
                            act.wait_ge(rope_done, g["rope"])
                        ins = high_parts(*pieces(g))
                    ins.then_inc(h_done, 1)
                elif ev == "M":
                    u = e["u"]
                    if new(max_done, u["n"] + 1):
                        act.wait_ge(max_done, u["n"] + 1)
                    if new(pt_done, u["e_free"]):
                        act.wait_ge(pt_done, u["e_free"])
                    r = u["n"] % 8
                    if u["branch"] == "swa":
                        scale = SCALE["swa"]
                    else:
                        i = 0 if u["branch"] == "mla" else u["h"]
                        scale = rq[:, i, u["tt"]:u["tt"] + 1]
                    nc.scalar.activation(e_of(u), wide[u["n"] % 2][:, u["lo"]:u["lo"] + u["width"]], ACT.Exp,
                                         bias=nbias[:, r:r + 1], scale=scale, accum_out=esum[:, r:r + 1]).then_inc(exp_done, 1)
                elif ev == "T":
                    t = e["t"]
                    if new(pt_done, t["n"] + 1):
                        act.wait_ge(pt_done, t["n"] + 1)
                    if t["n"] >= 2:
                        if new(pv_done, t["n"] - 1):
                            act.wait_ge(pv_done, t["n"] - 1)
                    nc.scalar.activation(pt_of(t, 0), ptp[t["n"] % 2][:, t["q0"] * P:t["q1"] * P], ACT.Copy).then_inc(pt_hi_ready, 1)
                elif ev == "O":
                    pa = e["pa"]
                    own, other = o_rows(pa)
                    if new(pv_done, pa["pt_end"]):
                        act.wait_ge(pv_done, pa["pt_end"])
                    if new(o_free, pa["o"]):
                        act.wait_ge(o_free, pa["o"])
                    nc.scalar.activation(o_half[own, 0:size(pa["tg"])], acc[1][other, 0:size(pa["tg"])], ACT.Copy).then_inc(o_copied, 1)
                elif ev == "XL":
                    if new(acc_done, e["acc"]):
                        act.wait_ge(acc_done, e["acc"])
                    if new(l_done, e["l_done"]):
                        act.wait_ge(l_done, e["l_done"])
                    if e["tail"] and e["l"] > 0:
                        if new(x_saved, 16):
                            act.wait_ge(x_saved, 16)
                    if e["l"] == 0:
                        act.dma_start(xres[:, 0:TT_CTX, :], t_in["ctx"][0, :, :].rearrange("(t p) d -> p t d", p=P)).then_inc(x_load, 16)
                        act.dma_start(xres[:, TT_CTX:TT, :], x_rows).then_inc(x_load, 16)
                    else:
                        act.dma_start(xres[:, TT_CTX:TT, :], x_mid.rearrange("(t p) d -> p t d", p=P)).then_inc(x_load, 16)
                        act.dma_start(fin_w[:, :], t_in["final_norm_w"].rearrange("(a d) -> a d", a=1).to_broadcast([P, D])).then_inc(fin_load, 16)
                    xl += 1
                elif ev == "TAB":
                    if new(acc_free, e["free"]):
                        act.wait_ge(acc_free, e["free"])
                    if new(rope_done, e["rope"]):
                        act.wait_ge(rope_done, e["rope"])
                    a, b = ("cos_m", "sin_m") if e["which"] == "m" else ("cos_s", "sin_s")
                    act.dma_start(cos[:, :], t_in[a]).then_inc(tab_load, 16)
                    act.dma_start(sin[:, :], t_in[b]).then_inc(tab_load, 16)
                elif ev in ("XN", "FN"):
                    tt = e["tt"]
                    if ev == "XN" and e["l"] == 0:
                        if new(x_load, 32):
                            act.wait_ge(x_load, 32)
                    else:
                        if new(xr_done, e["xr"]):
                            act.wait_ge(xr_done, e["xr"])
                    i = e["n"] + (LAYERS * TT if ev == "FN" else 0)
                    if ev == "XN":
                        if i >= 2:
                            if new(x_t, i - 1):
                                act.wait_ge(x_t, i - 1)
                    else:
                        if new(x_t, LAYERS * TT):
                            act.wait_ge(x_t, LAYERS * TT)
                        if e["n"] >= 2:
                            if new(out_saved[i % 2], 16 * (e["n"] // 2)):
                                act.wait_ge(out_saved[i % 2], 16 * (e["n"] // 2))
                    nc.scalar.activation(xn[:, i % 2, :], xres[:, tt, :], ACT.Square, accum_out=ssq[:, tt:tt + 1]).then_inc(x_sq, 1)
                    if new(x_sq, i + 1):
                        act.wait_ge(x_sq, i + 1)
                    nc.scalar.activation(rstd[:, tt:tt + 1], ssq[:, tt:tt + 1], ACT.Sqrt, scale=1.0 / D, bias=eps_col[:, 0:1]).then_inc(x_stat, 1)
                    if ev == "XN":
                        if new(x_b, i + 1):
                            act.wait_ge(x_b, i + 1)
                        nc.scalar.activation(h_hi[:, :, tt * P:(tt + 1) * P], x_mod[:, :].rearrange("p (k t) -> p k t", k=KD), ACT.Copy).then_inc(x_h, 1)
                    else:
                        if new(f_ready, e["n"] + 1):
                            act.wait_ge(f_ready, e["n"] + 1)
                        act.dma_start(out_rows[:, tt - TT_CTX, :], xn[:, i % 2, :]).then_inc(out_saved[i % 2], 16)
                elif ev == "XS":
                    if new(xr_done, e["xr"]):
                        act.wait_ge(xr_done, e["xr"])
                    act.dma_start(x_mid.rearrange("(t p) d -> p t d", p=P), xres[:, TT_CTX:TT, :]).then_inc(x_saved, 16)
            for i in range(2):
                if new(out_saved[i], 16 * (TT - TT_CTX) // 2):
                    act.wait_ge(out_saved[i], 16 * (TT - TT_CTX) // 2)
            if new(x_saved, 16):
                act.wait_ge(x_saved, 16)

        @block.gpsimd
        def _(pool):
            new = counting()
            link = splits = tiles = 0
            for e in events:
                ev = e["ev"]
                if ev == "W" and e["c"] < len(chunks):
                    c = e["c"]
                    k = chunk_size(c)
                    if new(w_hi_ready, c + 1):
                        pool.wait_ge(w_hi_ready, c + 1)
                    nc.gpsimd.tensor_tensor(w_lo[:, c % SPLIT_SLOTS, 0:k], w_raw[:, c % RAW_SLOTS, 0:k],
                                            f(w_hi[:, c % SPLIT_SLOTS, 0:k]), ALU.subtract).then_inc(w_lo_ready, 1)
                    splits += 1
                elif ev == "E" and e["g"].get("roped"):
                    g = e["g"]
                    if new(acc_free, g["v"]):
                        pool.wait_ge(acc_free, g["v"])
                    if new(tab_load, 32 * g["tab"]):
                        pool.wait_ge(tab_load, 32 * g["tab"])
                    if new(axt_ready, g["axt"]):
                        pool.wait_ge(axt_ready, g["axt"])
                    rows = slice(0, g["m"]) if g["kind"] != "kr" else slice(MLA_NOPE, MLA_K)
                    dst = lat_f[rows, 0, cols("x")] if g["kind"] == "ak" else rot[rows, :]
                    if g["kind"] == "kr":
                        if new(w_lo_ready, splits):
                            pool.wait_ge(w_lo_ready, splits)
                        if new(rope_done, g["rope"] - 1):
                            pool.wait_ge(rope_done, g["rope"] - 1)
                        if new(x_l, tiles):
                            pool.wait_ge(x_l, tiles)
                    link += 1
                    nc.gpsimd.tensor_tensor(swapped[rows, :], swapped[rows, :], sin[rows, :], ALU.mult).then_inc(rope_link, 1)
                    if new(rope_link, link):
                        pool.wait_ge(rope_link, link)
                    nc.gpsimd.tensor_tensor(dst, dst, swapped[rows, :], ALU.add).then_inc(rope_done, 1)
                    if g["kind"] == "kr":
                        if new(rope_done, g["rope"]):
                            pool.wait_ge(rope_done, g["rope"])
                elif ev == "XN":
                    tt = e["tt"]
                    if new(x_h, e["n"] + 1):
                        pool.wait_ge(x_h, e["n"] + 1)
                    ts = slice(tt * P, (tt + 1) * P)
                    nc.gpsimd.tensor_tensor(h_lo[:, :, ts], x_mod[:, :].rearrange("p (k t) -> p k t", k=KD), f(h_hi[:, :, ts]), ALU.subtract).then_inc(x_l, 1)
                    tiles += 1

        @block.vector
        def _(dve):
            new = counting()
            chain = [0]

            def link(ins):
                chain[0] += 1
                ins.then_inc(chain_v, 1)
                if new(chain_v, chain[0]):
                    dve.wait_ge(chain_v, chain[0])

            link(nc.vector.memset(eps_col[:, 0:1], EPS))
            link(nc.vector.memset(eps_col[:, 1:2], EPS / SCALE["mla"] ** 2))
            link(nc.vector.memset(eps_col[:, 2:3], EPS / SCALE["ax"] ** 2))
            if new(vec_done, 1):
                dve.wait_ge(vec_done, 1)
            link(nc.vector.tensor_copy(vec[:, :], acc[0][:, 0:V_ROWS]))
            link(nc.vector.stream_shuffle(vec_sw[:, :], vec[:, :], [i ^ 16 for i in range(32)]))
            if new(vec_load, 16 * VEC_LOADS):
                dve.wait_ge(vec_load, 16 * VEC_LOADS)
            link(nc.vector.memset(sink[:, :, 1], NEG))
            nc.vector.tensor_scalar(sink[:, :, 0], sink_in[:, :], 1.0 / SCALE["swa"], None, ALU.mult).then_inc(vec_ready, 1)
            if new(cs_th, 1):
                dve.wait_ge(cs_th, 1)
            link(nc.vector.scalar_tensor_tensor(cs_f[:, 1, :], cs_f[:, 0, :], 1.0, vec[:, 0:2 * KD], ALU.add, ALU.mult))
            link(nc.vector.tensor_scalar(cs_f[:, 0, :], cs_f[:, 1, :], 0.5, None, ALU.mult))
            silu = cs_f[:, 0, :].rearrange("p (s k) -> p k s", s=2)
            link(nc.vector.tensor_copy(cs[:, :, 0:2], silu))
            nc.vector.tensor_tensor(cs[:, :, 2:4], silu, f(cs[:, :, 0:2]), ALU.subtract).then_inc(cs_ready, 1)
            for e in events:
                ev = e["ev"]
                if ev == "E" and e["g"]["dve"]:
                    g = e["g"]
                    kind, src = g["kind"], acc[g["bank"]]
                    tg = g.get("tg")
                    N = size(tg) if tg else None
                    if new(acc_done, g["n"] + 1):
                        dve.wait_ge(acc_done, g["n"] + 1)
                    if g["act"]:
                        if new(ev_a, g["a"]):
                            dve.wait_ge(ev_a, g["a"])
                    if g.get("roped"):
                        if new(rope_done, g["rope_prev"][0]):
                            dve.wait_ge(rope_done, g["rope_prev"][0])
                        if new(l_done, g["rope_prev"][1]):
                            dve.wait_ge(l_done, g["rope_prev"][1])
                        if new(tab_load, 32 * g["tab"]):
                            dve.wait_ge(tab_load, 32 * g["tab"])
                        if new(axt_ready, g["axt"]):
                            dve.wait_ge(axt_ready, g["axt"])
                        pr = slice(0, g["m"])
                        rows = pr if kind != "kr" else slice(MLA_NOPE, MLA_K)
                        flip = 8 if kind in ("kr", "qm") else 16
                        dst = lat_f[rows, 0, cols("x")] if kind == "ak" else rot[rows, :]
                        nc.vector.stream_shuffle(swapped[rows, :], src[pr, 0:N], [i ^ flip for i in range(32)])
                        nc.vector.tensor_tensor(dst, src[pr, 0:N], cos[rows, :], ALU.mult).then_inc(acc_free, 1)
                    elif kind in DIRECT:
                        low_parts(*pieces(g)).then_inc(acc_free, 1)
                    elif kind == "ckv":
                        nc.vector.tensor_copy(lat_f[:, g["t"], cols(tg)], src[:, 0:N]).then_inc(acc_free, 1)
                    elif kind == "ak":
                        i = V_L + g["l"] * V_PER + V_AXK
                        nc.vector.tensor_scalar(lat_f[:, 0, cols(tg)], src[:, 0:N], vec[:, i:i + 1], None, ALU.mult).then_inc(acc_free, 1)
                    elif kind == "statb":
                        r = lat_r[:, cols(tg)]
                        nc.vector.reciprocal(r, r).then_inc(acc_free, 1)
                        if new(acc_free, g["v"]):
                            dve.wait_ge(acc_free, g["v"])
                        if g["what"] == "ak":
                            if new(rope_done, g["rope_done"]):
                                dve.wait_ge(rope_done, g["rope_done"])
                            x = lat_f[:, 0, cols(tg)]
                            ins = nc.vector.tensor_tensor(x, x, r, ALU.mult)
                        else:
                            i = V_L + g["l"] * V_PER + V_KVN
                            for t in range(KKV):
                                x = lat_f[:, t, cols(tg)]
                                ins = nc.vector.scalar_tensor_tensor(x, x, vec[:, i + t:i + t + 1], r, ALU.mult, ALU.mult)
                        ins.then_inc(stat_done, 1)
                    elif kind == "statq":
                        t0, t1 = g["tts"][0], g["tts"][-1] + 1
                        r = rq[:, 0, t0:t1] if g["what"] == "mla" else rq[:, g["head"]:g["head"] + 2, t0:t1]
                        nc.vector.reciprocal(r, r).then_inc(acc_free, 1)
                    elif kind == "z":
                        if new(o_free, g["o_done"]):
                            dve.wait_ge(o_free, g["o_done"])
                        t = th[:, g["th_slot"], 0:N]
                        o = o_t[:, g["t"], cols(tg)]
                        nc.vector.scalar_tensor_tensor(t, t, 1.0, src[:, 0:N], ALU.add, ALU.mult).then_inc(acc_free, 1)
                        if new(acc_free, g["v"]):
                            dve.wait_ge(acc_free, g["v"])
                        nc.vector.scalar_tensor_tensor(o, t, 0.5, o, ALU.mult, ALU.mult).then_inc(th_done, 1)
                    elif kind == "y":
                        if new(ev_a, g["of"]["a"]):
                            dve.wait_ge(ev_a, g["of"]["a"])
                        t = th[:, g["of"]["th_slot"], 0:N]
                        y = y2[:, g["t"], cols(tg)]
                        if g["branch"] == BRANCHES[0]:
                            nc.vector.scalar_tensor_tensor(y, t, 1.0, src[:, 0:N], ALU.add, ALU.mult).then_inc(acc_free, 1)
                        else:
                            nc.vector.scalar_tensor_tensor(t, t, 1.0, src[:, 0:N], ALU.add, ALU.mult).then_inc(acc_free, 1)
                            if new(acc_free, g["v"]):
                                dve.wait_ge(acc_free, g["v"])
                            nc.vector.tensor_tensor(y, y, t, ALU.add).then_inc(th_done, 1)
                    elif kind == "ada":
                        nc.vector.tensor_copy(a_row[0:4, g["slot"], :], src[0:4, 0:256]).then_inc(acc_free, 1)
                    elif kind == "adaT":
                        nc.vector.tensor_copy(mod_col[:, 2 * g["j"]:2 * g["j"] + 2, :],
                                              src[:, 0:4].rearrange("p (b s) -> p b s", b=2)).then_inc(acc_free, 1)
                    elif kind == "adaG":
                        c0 = (g["j"] - 2 * D // 256) * 256
                        which = 0 if g["s"] == 0 else 1
                        nc.vector.tensor_copy(gate[:, which, c0:c0 + 256], src[:, 0:256]).then_inc(acc_free, 1)
                    elif kind == "wout":
                        s = 0 if g["tt"] >= TT_CTX else 1
                        if new(x_load, 16 * X_LOADS[g["l"]]):
                            dve.wait_ge(x_load, 16 * X_LOADS[g["l"]])
                        if new(acc_free, g["gates"]):
                            dve.wait_ge(acc_free, g["gates"])
                        if new(xr_done, g["xr"] - 1):
                            dve.wait_ge(xr_done, g["xr"] - 1)
                        c = slice(g["j"] * 256, (g["j"] + 1) * 256)
                        nc.vector.tensor_tensor(x_add[:, :], src[:, 0:256], gate[:, s, c], ALU.mult).then_inc(acc_free, 1)
                        if new(acc_free, g["v"]):
                            dve.wait_ge(acc_free, g["v"])
                        x = xres[:, g["tt"], c]
                        nc.vector.tensor_tensor(x, x, x_add[:, :], ALU.add).then_inc(xr_done, 1)
                elif ev == "L":
                    g = e["g"]
                    if new(h_done, g["high_n"]):
                        dve.wait_ge(h_done, g["high_n"])
                    if g["kind"] == "z":
                        o = o_t[:, g["t"], cols(g["tg"])]
                        ins = nc.vector.tensor_tensor(og_lo[:, g["t"], cols(g["tg"])], o, f(og_hi[:, g["t"], cols(g["tg"])]), ALU.subtract)
                    elif g["kind"] == "y":
                        c = cols(g["tg"])
                        ins = nc.vector.scalar_tensor_tensor(y_lo[:, g["t"], c], y2[:, g["t"], c], 0.5, f(y_hi[:, g["t"], c]), ALU.mult, ALU.subtract)
                    else:
                        ins = low_parts(*pieces(g))
                    ins.then_inc(l_done, 1)
                elif ev == "M":
                    u = e["u"]
                    r = u["n"] % 8
                    if new(s_done, u["n"] + 1):
                        dve.wait_ge(s_done, u["n"] + 1)
                    if u["n"] >= 8:
                        if new(exp_done, u["n"] - 7):
                            dve.wait_ge(exp_done, u["n"] - 7)
                    link(nc.vector.tensor_reduce(nmax[:, r:r + 1], wide[u["n"] % 2][:, u["lo"]:u["lo"] + u["width"]], AX.X, ALU.max, negate=True))
                    if u["branch"] == "swa":
                        scale = SCALE["swa"]
                    else:
                        i = 0 if u["branch"] == "mla" else u["h"]
                        scale = rq[:, i, u["tt"]:u["tt"] + 1]
                    nc.vector.tensor_scalar(nbias[:, r:r + 1], nmax[:, r:r + 1], scale, None, ALU.mult).then_inc(max_done, 1)
                elif ev == "N":
                    u = e["u"]
                    r = u["n"] % 8
                    if new(exp_done, u["n"] + 1):
                        dve.wait_ge(exp_done, u["n"] + 1)
                    link(nc.vector.reciprocal(einv[:, r:r + 1], esum[:, r:r + 1]))
                    nc.vector.tensor_scalar(e_of(u), e_of(u), einv[:, r:r + 1], None, ALU.mult).then_inc(norm_done, 1)
                elif ev == "T":
                    t = e["t"]
                    if new(pt_hi_ready, t["n"] + 1):
                        dve.wait_ge(pt_hi_ready, t["n"] + 1)
                    nc.vector.tensor_tensor(pt_of(t, 1), ptp[t["n"] % 2][:, t["q0"] * P:t["q1"] * P], f(pt_of(t, 0)), ALU.subtract).then_inc(pt_lo_ready, 1)
                elif ev == "O":
                    pa = e["pa"]
                    own, _ = o_rows(pa)
                    if new(o_copied, pa["o"] + 1):
                        dve.wait_ge(o_copied, pa["o"] + 1)
                    k = size(pa["tg"])
                    nc.vector.tensor_tensor(o_t[own, pa["h"] // 2, cols(pa["tg"])], acc[1][own, 0:k], o_half[own, 0:k], ALU.add).then_inc(o_free, 1)
                elif ev == "MOD":
                    if new(acc_free, e["free"]):
                        dve.wait_ge(acc_free, e["free"])
                    i = V_L + e["l"] * V_PER + V_NORM
                    for s in range(2):
                        ins = nc.vector.scalar_tensor_tensor(mod_a[:, s, :], mod_col[:, KD:2 * KD, s], 1.0, vec[:, i:i + KD], ALU.add, ALU.mult)
                    ins.then_inc(mod_ready, 1)
                elif ev == "AXT":
                    if new(tab_load, 32 * e["tab"]):
                        dve.wait_ge(tab_load, 32 * e["tab"])
                    i = V_L + e["l"] * V_PER + e["which"]
                    nc.vector.tensor_scalar(cos[:, :], cos[:, :], vec[:, i:i + 1], None, ALU.mult)
                    nc.vector.tensor_scalar(sin[:, :], sin[:, :], vec_sw[:, i:i + 1], None, ALU.mult).then_inc(axt_ready, 1)
                elif ev in ("XN", "FN"):
                    tt = e["tt"]
                    i = e["n"] + (LAYERS * TT if ev == "FN" else 0)
                    s = 0 if tt >= TT_CTX else 1
                    if new(x_stat, i + 1):
                        dve.wait_ge(x_stat, i + 1)
                    link(nc.vector.reciprocal(rstd[:, tt:tt + 1], rstd[:, tt:tt + 1]))
                    if ev == "FN":
                        if new(fin_load, 16):
                            dve.wait_ge(fin_load, 16)
                        nc.vector.scalar_tensor_tensor(xn[:, i % 2, :], xres[:, tt, :], rstd[:, tt:tt + 1], fin_w[:, :], ALU.mult, ALU.mult).then_inc(f_ready, 1)
                    else:
                        nc.vector.tensor_scalar(xn[:, i % 2, :], xres[:, tt, :], rstd[:, tt:tt + 1], None, ALU.mult).then_inc(x_n, 1)
                        if new(x_t, i + 1):
                            dve.wait_ge(x_t, i + 1)
                        if new(mod_ready, e["mod"]):
                            dve.wait_ge(mod_ready, e["mod"])
                        if i:
                            if new(x_l, i):
                                dve.wait_ge(x_l, i)
                        m = x_mod[:, :].rearrange("p (k t) -> p k t", k=KD)
                        w = wide[i % 2][:, :].rearrange("p (k t) -> p k t", k=KD)
                        nc.vector.tensor_tensor(m, w, mod_a[:, s, :].unsqueeze(2).to_broadcast([P, KD, P]), ALU.mult).then_inc(x_f, 1)
                        if new(x_f, i + 1):
                            dve.wait_ge(x_f, i + 1)
                        nc.vector.tensor_tensor(m, m, mod_col[:, 0:KD, s].unsqueeze(2).to_broadcast([P, KD, P]), ALU.add).then_inc(x_b, 1)


def constants():
    import numpy as np
    pos = np.arange(SEQ)
    rows, colsp = (pos // GRID_W).astype(np.float32), (pos % GRID_W).astype(np.float32)

    def table(quarter):
        d = 2 * quarter
        freq = np.float32(THETA) ** (-np.arange(0, d, 2, dtype=np.float32) / np.float32(d))
        cs, sn = [], []
        for p in (rows, colsp):
            ang = (p[:, None] * freq[None, :]).astype(np.float32)
            cs += [np.cos(ang).T, np.cos(ang).T]
            sn += [-np.sin(ang).T, np.sin(ang).T]
        return np.concatenate(cs).astype(np.float32), np.concatenate(sn).astype(np.float32)

    c64, s64 = table(HD // 4)
    c32, s32 = table(MLA_ROPE // 4)
    out = {"cos_s": np.tile(c64, (2, 1)), "sin_s": np.tile(s64, (2, 1))}
    cm, sm = np.ones((P, SEQ), np.float32), np.zeros((P, SEQ), np.float32)
    cm[MLA_NOPE:MLA_K], sm[MLA_NOPE:MLA_K] = c32, s32
    out["cos_m"], out["sin_m"] = cm, sm
    k = np.zeros((P, K_END), np.float32)
    i, j = np.arange(P)[:, None], np.arange(P)[None, :]
    k[:, K_ID:K_ID + P] = i == j
    k[:, K_ONE:K_ONE + P] = 1.0
    k[:, K_BLK:K_BLK + P] = (i // HD) == (j // HD)
    k[:, K_MPREV:K_MPREV + P] = np.where(j >= i, 0.0, NEG)
    k[:, K_MNEXT:K_MNEXT + P] = np.where(j <= i, 0.0, NEG)
    k[[0, 2, 4], K_SEL] = 1.0
    k[[1, 3, 4], K_SEL + 1] = 1.0
    out["consts"] = k
    return out


INPUTS = ["x", "c", "ctx", "c_ctx", "ada_w", "ada_b", "norm_w", "w_in", "mla_q_norm", "mla_w_uq", "mla_kv_norm", "mla_w_ukv",
          "swa_sink", "ax_q_norm", "ax_k_norm", "w_o_mla", "w_o_swa", "w_o_ax", "w_out", "final_norm_w"]


def kernel(**inputs):
    import numpy as np
    import concourse.bacc as bacc
    from concourse.bass_utils import run_bass_kernel_spmd

    nc = bacc.Bacc("TRN2", target_bir_lowering=False, num_devices=1)
    arrays, t_in = {}, {}
    for name, a in list((k, inputs[k]) for k in INPUTS) + list(constants().items()):
        a = np.ascontiguousarray(a)
        arrays["in_" + name] = a
        t_in[name] = nc.dram_tensor("in_" + name, list(a.shape), mybir.dt.float32, kind="ExternalInput").ap()
    out = nc.dram_tensor("out_x", [1, SEQ, D], mybir.dt.float32, kind="ExternalOutput").ap()
    build(nc, t_in, out)
    r = run_bass_kernel_spmd(nc, [arrays], core_ids=[0])
    return r.results[0]["out_x"]
```

```python
import concourse.bass as bass
from concourse import mybir
from contextlib import ExitStack

D = 1024
CTX, SEQ = 256, 512
TOK = CTX + SEQ
LAYERS = 2
P = 128
KD = D // P
TT_CTX, TT = CTX // P, TOK // P
HEADS, KVH, HD = 8, 2, 64
MLA_NOPE, MLA_ROPE, MLA_V = 64, 32, 64
MLA_K = MLA_NOPE + MLA_ROPE
Q_RANK, KV_RANK = 384, 256
KQ, KKV = Q_RANK // P, KV_RANK // P
WIDTH = HEADS * HD
KO = WIDTH // P
WINDOW = 128
EPS = 1e-6
NEG = -1e30
GRID_W, THETA = 64, 10000.0
C_CKV, C_KR = 0, 256
C_SK, C_SV, C_AK, C_AV = 288, 416, 544, 672
C_CQ = 800
C_Q = {"swa": 1184, "ax": 1696}
C_Z = {"mla": 2208, "swa": 2720, "ax": 3232}
C_G = {"mla": 3744, "swa": 4768, "ax": 5792}
BRANCHES = ("mla", "swa", "ax")
SCALE = {"mla": float(MLA_K) ** -0.5, "swa": float(HD) ** -0.5, "ax": float(HD) ** -0.5}

V_C, V_CC = 0, KD
V_L = 2 * KD
V_NORM, V_QN, V_KVN, V_AXQ, V_AXK = 0, KD, KD + KQ, KD + KQ + KKV, KD + KQ + KKV + 1
V_PER = KD + KQ + KKV + 2
V_ROWS = V_L + LAYERS * V_PER

K_ID, K_ONE, K_BLK, K_MPREV, K_MNEXT, K_SEL, K_END = 0, 128, 256, 384, 512, 640, 642

CHUNK = 1024
RAW_SLOTS, SPLIT_SLOTS = 3, 4


def tokens(group):
    return (0, CTX) if group == "c" else (CTX, SEQ)
E_UNITS = 5


def token_groups(l):
    return ("x", "c") if l + 1 < LAYERS else ("x",)


def token_tiles(l):
    return list(range(TT)) if l + 1 < LAYERS else list(range(TT_CTX, TT))


def key_tiles(units):
    tiles, used = [], 4
    for kt in sorted({k for u in units for k in u["kts"]}):
        q = [i for i, u in enumerate(units) if kt in u["kts"]]
        if used + len(q) > 4:
            tiles.append([])
            used = 0
        tiles[-1].append((kt, q[0], q[-1] + 1, used))
        used += len(q)
    return tiles


def passes(l, branch):
    out = []
    for h in range(HEADS):
        for tt0 in list(range(TT_CTX, TT, 2)) + ([0] if "c" in token_groups(l) else []):
            tg, units = ("x" if tt0 else "c"), []
            for tt in (tt0, tt0 + 1):
                masks, lo = [], 0
                if branch != "swa":
                    pieces = [(0, 0, 512), (512, 512, TOK - 512)] if tg == "x" else [(0, 0, CTX)]
                    width = TOK if tg == "x" else CTX
                    kts = {k: k * P for k in range(width // P)}
                else:
                    lo, pieces, kts = 254, [(256, 0, CTX)], {0: 2, 1: 2 + P}
                    width = 2 + CTX
                    if tg == "x":
                        q = tt - TT_CTX
                        k0, k1 = max(q - 1, 0), min(q + 2, SEQ // P)
                        pieces.append((512, CTX + k0 * P, (k1 - k0) * P))
                        masks = [(512 + (k - k0) * P, 0 if k < q else 1) for k in range(k0, k1) if k != q]
                        kts.update({TT_CTX + k: 2 + CTX + (k - k0) * P for k in range(k0, k1)})
                        width += (k1 - k0) * P
                units.append(dict(l=l, branch=branch, h=h, tt=tt, pieces=pieces, masks=masks, kts=kts, lo=lo, width=width))
            out.append(dict(l=l, branch=branch, h=h, units=units, tiles=key_tiles(units)))
    return out


def schedule():
    events, chunks, later = [], [], []
    n = dict(acc=0, ev_a=0, free=0, rope=0, stat=0, h=0, l=0, th=0, s=0, pt=0, o=0, x=0, f=0, xr=0, mod=0,
             split=0, tab=0, axt=0, ada=0, xl=0)
    bank_last = {0: None, 1: None}
    chunk_last, th_last = {}, {0: None, 1: None}
    turn = [0]

    def emit(ev, **e):
        events.append(dict(ev=ev, **e))

    def tick():
        for item in list(later):
            item[0] -= 1
            if item[0] <= 0:
                later.remove(item)
                item[1]()

    def flush():
        while later:
            later.pop(0)[1]()

    def bank():
        turn[0] ^= 1
        return turn[0]

    def chunk(kind, *where):
        chunks.append((kind,) + where)
        return len(chunks) - 1

    def group(kind, bank_no, parts=1, chunk_ids=(), oldest=None, hl=False, needs=None, act=True, dve=True, **kw):
        g = dict(kind=kind, bank=bank_no, chunks=list(chunk_ids), parts=parts, act=act, dve=dve, hl=hl, **kw)

        def step(part):
            def run():
                if part == 0:
                    g.update(n=n["acc"], before=bank_last[bank_no], passes=n["o"], needs=needs() if needs else {})
                    n["acc"] += 1
                    bank_last[bank_no] = g
                    if chunk_ids:
                        while n["split"] < (chunk_ids[0] if oldest is None else oldest) + SPLIT_SLOTS:
                            c = n["split"]
                            emit("W", c=c, reuse=chunk_last.get(c - SPLIT_SLOTS, 0))
                            n["split"] += 1
                    for c in chunk_ids:
                        chunk_last[c] = g["n"] + 1
                emit("G", g=g, part=part)
                if part == parts - 1:
                    read_out()
                tick()
            return run

        def read_out():
            if g.get("roped"):
                flush()
                g["rope_prev"] = (n["rope"], n["l"])
                n["rope"] += 1
                g["rope"], g["tab"], g["axt"] = n["rope"], n["tab"], n["axt"]
            if act:
                n["ev_a"] += 1
                g["a"] = n["ev_a"]
            if dve:
                n["free"] += 1
                g["v"] = n["free"]
            if kind == "statb":
                n["stat"] += 1
                g["stat"] = n["stat"]
            if kind in ("z", "g"):
                g["th_slot"] = 0 if g["tg"] == "x" else 1
                g["th_before"] = th_last[g["th_slot"]]
            if kind == "z" or (kind == "y" and g["branch"] != BRANCHES[0]):
                n["th"] += 1
                g["th"] = n["th"]
            if kind == "z":
                th_last[g["th_slot"]] = g
            if kind == "y":
                th_last[g["of"]["th_slot"]] = g
            if kind == "wout":
                n["xr"] += 1
                g["xr"] = n["xr"]
            if kind == "ada":
                n["ada"] += 1
            emit("E", g=g)
            if hl:
                later.append([1, high])

        def high():
            n["h"] += 1
            g["high_n"] = n["h"]
            emit("H", g=g)
            later.append([1, low])

        def low():
            n["l"] += 1
            g["low_n"] = n["l"]
            emit("L", g=g)

        g["steps"] = [step(p) for p in range(parts)]
        return g

    def go(g):
        for s in g["steps"]:
            s()
        return g

    def project(kind, l, c, tg, bank_no, parts=1, src="h", co=0, m=P, width=P, k=KD, needs=None, **kw):
        need = needs or (lambda x=n["x"]: dict(x_l=x))
        return group(kind, bank_no, parts, (c,), l=l, mode="w", src=src, co=co, m=m, width=width, k=k, tg=tg, needs=need, **kw)

    def roped(tg, squares=False):
        return dict(roped=True, hl=True, act=squares) if tg == "x" else dict(roped=False)

    def load_table(which):
        flush()
        emit("TAB", which=which, free=n["free"], rope=n["rope"])
        n["tab"] += 1

    def attention(l, branch, items, span, ready, ready_v):
        ps = passes(l, branch)
        units, tiles, owner = [], [], {}
        for pa in ps:
            blocks = pa["tiles"]
            pa["tiles"] = [dict(n=n["pt"] + j, blocks=b, pa=pa, first=j == 0, last=j == len(blocks) - 1, ready_v=ready_v,
                                width=(b[-1][3] + b[-1][2] - b[-1][1]) * P) for j, b in enumerate(blocks)]
            n["pt"] += len(blocks)
            pa.update(pt_end=n["pt"], o=n["o"], done=False, normed=0)
            n["o"] += 1
            for u in pa["units"]:
                u["pa"] = pa
            units += pa["units"]
            tiles += pa["tiles"]
        coming, wait_x, wait_m, wait_n = list(units), [], [], []
        steps, pace, valued = [], 1, 0

        def S(u):
            if any(g["hl"] and "low_n" not in g for g in ready[u["h"]]):
                flush()
            u.update(n=n["s"], slot=n["s"] % E_UNITS, x=n["x"],
                     ready_free=max(g["v"] for g in ready[u["h"]]), ready_l=max(g.get("low_n", 0) for g in ready[u["h"]]))
            n["s"] += 1
            emit("S", u=u)

        def M(u):
            before = owner.get(u["slot"])
            u["e_free"] = before["pt_end"] if before else 0
            owner[u["slot"]] = u["pa"]
            emit("M", u=u)

        def N(u):
            emit("N", u=u)
            u["pa"]["normed"] += 1

        def maximum():
            if wait_x:
                emit("X", u=wait_x[0])
                wait_m.append(wait_x.pop(0))

        def advance():
            took = moved = False
            if coming and len(wait_m) + len(wait_x) < 2 and all("v" in g for g in ready.get(coming[0]["h"], [{}])):
                wait_x.append(coming.pop(0))
                S(wait_x[-1])
                took = True
            if wait_m and owner.get(wait_m[0]["slot"], dict(done=True))["done"]:
                wait_n.append(wait_m.pop(0))
                M(wait_n[-1])
                took = moved = True
            if wait_n and (len(wait_n) > 1 or not moved):
                N(wait_n.pop(0))
                took = True
            tick()
            return took

        def fill():
            nonlocal pace
            if not steps and items and not any(u["h"] == items[0][0] for u in coming) and valued >= items[0][1]:
                steps.extend(items.pop(0)[2]())
                pace = -(-len(steps) // span)
            if steps:
                steps.pop(0)()

        def value(t):
            assert all("v" in g for g in t["ready_v"][t["pa"]["h"] // 2])
            nonlocal valued
            t.update(values=max(g["v"] for g in t["ready_v"][t["pa"]["h"] // 2]), bank1=bank_last[1])
            emit("PV", t=t)
            valued = t["pa"]["h"]

        finished = None
        for i, t in enumerate(tiles):
            pa = t["pa"]
            while pa["normed"] < len(pa["units"]):
                maximum()
                if not advance():
                    fill()
            maximum()
            if finished:
                emit("O", pa=finished)
                finished = None
            emit("T", t=t)
            pa["done"] = t["last"]
            advance()
            fill()
            if i > 0:
                value(tiles[i - 1])
                if tiles[i - 1]["last"]:
                    finished = tiles[i - 1]["pa"]
            for _ in range(pace - 1):
                fill()
        while steps:
            steps.pop(0)()
        value(tiles[-1])
        if finished:
            emit("O", pa=finished)
        emit("O", pa=ps[-1])

    def ada(l, j):
        slot = n["ada"] % 2
        cc = (chunk("ada", l, j, 0, slot, ada_reader[slot]), chunk("ada", l, j, 1))
        steps = list(group("ada", bank_for(), parts=2, chunk_ids=cc, act=False, mode="ada", l=l, j=j, slot=slot,
                           needs=lambda: dict(cs_ready=1))["steps"])
        shape = dict(act=False, l=l, j=j, slot=slot, needs=lambda: dict(acc_free=n["free"], loads=(n["ada"] + 1) // 2))
        if j < 2 * D // 256:
            steps += group("adaT", bank_for(), mode="adaT", **shape)["steps"]
        else:
            for s in range(len(token_groups(l))):
                steps += group("adaG", bank_for(), mode="adaG", s=s, **shape)["steps"]

        def read():
            ada_reader[slot] = n["acc"]
            if j == 2 * D // 256 - 1:
                emit("MOD", l=l, free=n["free"])
                n["mod"] += 1
        return steps + [read]

    COLUMNS, GATES = range(2 * D // 256), range(2 * D // 256, 3 * D // 256)
    fixed_bank = []

    def bank_for():
        return fixed_bank[0] if fixed_bank else bank()

    ada_reader = {0: 0, 1: 0}

    def z_and_merge(l, b):
        branch = BRANCHES[b]
        for t in range(KO):
            c = chunk("win", l, C_Z[branch] + t * P, P)
            for tg in token_groups(l):
                go(project("z", l, c, tg, bank(), branch=branch, t=t, hl=True, o_done=n["o"]))
        flush()
        og = n["l"]
        for t in range(KD):
            cg, cy = chunk("win", l, C_G[branch] + t * P, P), chunk("wo", l, b, t)
            gates = {tg: go(project("g", l, cg, tg, bank(), branch=branch, t=t, dve=False)) for tg in token_groups(l)}
            for tg in token_groups(l):
                go(project("y", l, cy, tg, bank(), src="og", k=KO, branch=branch, t=t, of=gates[tg], hl=(b == 2), act=False,
                           needs=lambda og=og: dict(l_done=og)))
            if b == 2 and t % (KD // len(GATES)) == 0:
                for s in ada(l, GATES[t // (KD // len(GATES))]):
                    s()
        flush()

    def norm_rows(l, tt, xr):
        emit("XN", l=l, tt=tt, n=n["x"], s=n["s"], xr=xr, xl=n["xl"])
        n["x"] += 1

    def modulate_rows(tt):
        emit("XM", tt=tt, n=n["x"] - 1 if tt == TT - 1 else n["x"] - 2, mod=n["mod"])

    def next_norm(l, added, i):
        if i < 0:
            return
        tt, xr = added[i]
        if l + 1 < LAYERS:
            norm_rows(l + 1, tt, xr)
            if i > 0:
                modulate_rows(added[i - 1][0])
        else:
            emit("FN", tt=tt, n=n["f"], xr=xr)
            n["f"] += 1

    for l in range(LAYERS):
        tgs, tts = token_groups(l), token_tiles(l)
        if l == 0:
            emit("XL", l=0, tail=False, acc=0, l_done=0, h=0, rope=0)
            n["xl"] += 1
            for j in COLUMNS:
                for s in ada(0, j):
                    s()
            for tt in range(TT):
                norm_rows(0, tt, 0)
                if tt > 0:
                    modulate_rows(tt - 1)
            modulate_rows(TT - 1)

        load_table("m")
        cks = [chunk("win", l, C_CKV + t * P, P) for t in range(KKV)]
        for t in range(KKV):
            for tg in ("x", "c"):
                go(project("ckv", l, cks[t], tg, bank(), t=t))
        c = chunk("win", l, C_KR, MLA_ROPE)
        for tg in ("x", "c"):
            go(project("kr", l, c, tg, bank(), m=MLA_ROPE, width=MLA_ROPE, what="kr", **roped(tg)))
        for tg in ("x", "c"):
            go(group("statb", bank(), mode="statb", l=l, tg=tg, what="ckv", hl=True, tiles=KKV, nsum=KV_RANK, needs=lambda: dict(ev_a=n["ev_a"])))
        for t in range(KQ):
            c = chunk("win", l, C_CQ + t * P, P)
            for tg in tgs:
                go(project("cq", l, c, tg, bank(), what="cq", t=t))
        flush()
        go(group("statq", bank(), mode="statq", l=l, what="mla", tts=tts, tiles=KQ, needs=lambda: dict(ev_a=n["ev_a"])))
        latents = dict(acc_free=n["free"], l_done=n["l"])
        ready, ready_v, steps = {}, {}, {}

        def mla_pair(p, bank_of, parts):
            cq, ck = chunk("uq", l, p), chunk("ukv", l, p)
            for h in (2 * p, 2 * p + 1):
                gs = [project("qm", l, cq, tg, bank_of(), parts, src="cq", co=(h % 2) * MLA_K, m=MLA_K, width=2 * MLA_K, k=KQ,
                              needs=lambda: latents, what="qm", head=h, **roped(tg)) for tg in tgs]
                ready[h] = gs
                steps[h] = [s for g in gs for s in g["steps"]]
            for h in (2 * p, 2 * p + 1):
                gs = [project("km", l, ck, tg, bank_of(), parts, src="ckv", oldest=cq, co=(h % 2) * P, m=MLA_NOPE, width=2 * P, k=KKV,
                              needs=lambda: latents, what="km", head=h) for tg in ("x", "c")]
                ready[h] = ready[h] + gs
                steps[h] += [s for g in gs for s in g["steps"]]
            ready_v[p] = [group("vm", bank_of(), chunk_ids=(ck,), oldest=cq, parts=2, mode="vm", l=l,
                                tts=range(tt, tt + 3), what="vm", pair=p, needs=lambda: latents) for tt in range(0, TT, 3)]
            steps[2 * p] += [s for g in ready_v[p] for s in g["steps"]]

        mla_pair(0, bank, 1)
        for h in (0, 1):
            for s in steps[h]:
                s()
        flush()

        def mla_head(h):
            def make():
                if h % 2 == 0:
                    mla_pair(h // 2, lambda: 0, 2)
                return list(steps[h])
            return (h - 2, h - 2, make)

        attention(l, "mla", [mla_head(h) for h in range(2, HEADS)], 5, ready, ready_v)
        flush()
        ada_reader.update({0: n["acc"], 1: n["acc"]})
        z_and_merge(l, 0)

        load_table("s")
        c = chunk("win", l, C_SK, P)
        keys = [go(project("ks", l, c, tg, bank(), what="k", **roped(tg))) for tg in ("x", "c")]
        cc = (chunk("v", l, 0), chunk("v", l, 1))
        values = [go(group("vs", bank(), chunk_ids=cc, mode="vs", l=l, tts=range(tt, tt + 2), what="vs",
                           needs=lambda: dict(x_l=n["x"]))) for tt in range(0, TT, 2)]
        flush()
        for branch in ("swa", "ax"):
            if branch == "ax":
                load_table("s")
                emit("AXT", l=l, which=V_AXK, tab=n["tab"])
                n["axt"] += 1
                c = chunk("win", l, C_AK, P)
                for tg in ("x", "c"):
                    go(project("ak", l, c, tg, bank(), roped=(tg == "x")))
                keys = [go(group("statb", bank(), mode="statb", l=l, tg=tg, what="ak", hl=True, tiles=1, nsum=HD,
                                 needs=lambda: dict(ev_a=n["ev_a"]), rope_done=n["rope"])) for tg in ("x", "c")]
                load_table("s")
                emit("AXT", l=l, which=V_AXQ, tab=n["tab"])
                n["axt"] += 1
            ready, ready_v = {}, {p: values for p in range(HEADS // 2)}

            def q_pair(t, bank_of, parts):
                c = chunk("win", l, C_Q[branch] + t * P, P)
                gs = [project("qs", l, c, tg, bank_of(), parts, what="qs", head=2 * t, branch=branch,
                              **roped(tg, squares=branch == "ax")) for tg in tgs]
                if branch == "ax":
                    gs.append(group("statq", bank_of(), mode="statq", l=l, what="ax", head=2 * t, tts=tts, tiles=1, needs=lambda: dict(ev_a=n["ev_a"])))
                for h in (2 * t, 2 * t + 1):
                    ready[h] = gs + keys
                return [s for g in gs for s in g["steps"]]

            for s in q_pair(0, bank, 1):
                s()
            flush()

            items = [(2 * t - 3, 0, lambda t=t: q_pair(t, lambda: 0, 3)) for t in range(1, HEADS // 2)]
            if branch == "ax" and l + 1 < LAYERS:
                more = [(-1, 0, lambda j=j: ada(l + 1, j)) for j in COLUMNS]
                items = items[:1] + more[:2] + items[1:2] + more[2:5] + items[2:] + more[5:]
            fixed_bank.append(0)
            attention(l, branch, items, 8, ready, ready_v)
            while items:
                for s in items.pop(0)[2]():
                    s()
            fixed_bank.clear()
            flush()
            z_and_merge(l, BRANCHES.index(branch))

        y_ready = n["l"]
        emit("XL", l=l, tail=True, acc=n["acc"], l_done=n["l"], h=n["h"], rope=n["rope"])
        n["xl"] += 1
        gates = n["free"]
        added = []
        for j in range(D // 256):
            cc = (chunk("wout", l, j, 0), chunk("wout", l, j, 1))
            for i, tt in enumerate(tts):
                g = go(group("wout", bank(), chunk_ids=cc, act=False, mode="wout", l=l, j=j, tt=tt, xl=n["xl"],
                             gates=gates, needs=lambda: dict(l_done=y_ready)))
                if j == D // 256 - 1:
                    added.append((tt, g["xr"]))
                    next_norm(l, added, i - 1)
        next_norm(l, added, len(added) - 1)
        if l + 1 < LAYERS:
            modulate_rows(tts[-1])
            emit("XS", l=l, xr=n["xr"])
    return events, chunks


def build(nc, t_in, out):
    F, R = mybir.dt.float32, mybir.dt.float32r
    ALU, ACT, AX = mybir.AluOpType, mybir.ActivationFunctionType, mybir.AxisListType
    events, chunks = schedule()
    x_mid = nc.dram_tensor("x_mid", [SEQ, D], F, kind="Internal").ap()

    base = [(nc.sbuf_base + 31) // 32 * 32]

    def fixed(name, shape, dt):
        size = 4
        for s in shape[1:]:
            size *= s
        t = nc.alloc_sbuf_tensor_at(name, shape, dt, offset=base[0])
        base[0] += (size + 31) // 32 * 32
        return t

    h_hi, h_lo = fixed("h_hi", [P, KD, TOK], R), fixed("h_lo", [P, KD, TOK], R)
    w_raw = fixed("w_raw", [P, RAW_SLOTS, CHUNK], F)
    w_hi, w_lo = fixed("w_hi", [P, SPLIT_SLOTS, CHUNK], R), fixed("w_lo", [P, SPLIT_SLOTS, CHUNK], R)
    cos, sin = fixed("cos", [P, SEQ], F), fixed("sin", [P, SEQ], F)
    swapped, rot = fixed("swapped", [P, SEQ], F), fixed("rot", [P, SEQ], F)
    o_half = fixed("o_half", [P, SEQ], F)
    ident, ones, blk = fixed("ident", [P, P], F), fixed("ones", [P, P], F), fixed("blk", [P, P], F)
    ident_r, mask_r = fixed("ident_r", [P, P], R), fixed("mask_r", [P, 2, P], R)
    sel = fixed("sel", [5, 2], F)
    vec, vec_sw = fixed("vec", [P, V_ROWS], F), fixed("vec_sw", [P, V_ROWS], F)
    cs = fixed("cs", [P, KD, 4], R)
    cs_f = fixed("cs_f", [P, 2, 2 * KD], F)
    mod_col, mod_a = fixed("mod_col", [P, 2 * KD, 2], F), fixed("mod_a", [P, 2, KD], F)
    rq = fixed("rq", [P, HEADS, TT], F)
    nmax, nbias, esum, einv = (fixed(k, [P, 8], F) for k in ("nmax", "nbias", "esum", "einv"))
    ssq, rstd = fixed("ssq", [P, TT], F), fixed("rstd", [P, TT], F)
    sink_in, sink = fixed("sink_in", [1, LAYERS * HEADS], F), fixed("sink", [1, LAYERS * HEADS, 2], F)
    eps_col = fixed("eps_col", [P, 3], F)
    start = base[0]
    ends = []

    def shared(name, shape, dt, at):
        size = 4
        for s in shape[1:]:
            size *= s
        ends.append(start + at + size)
        return nc.alloc_sbuf_tensor_at(name, shape, dt, offset=start + at)

    FEAT = TOK * 4
    y2, y_lo = shared("y2", [P, KD, TOK], F, 0), shared("y_lo", [P, KD, TOK], R, 0)
    o_t = shared("o_t", [P, KO, TOK], F, 24576)
    og_hi, og_lo = shared("og_hi", [P, KO, TOK], R, 36864), shared("og_lo", [P, KO, TOK], R, 49152)
    th = shared("th", [P, 2, SEQ], F, 61440)
    y_hi = shared("y_hi", [P, KD, TOK], R, 65536)
    q_m = shared("q_m", [P, 2, 2, TOK], R, 36864)
    q_s = shared("q_s", [P, 4, TOK], R, 36864)
    e_m = shared("e_m", [P, E_UNITS, TOK], F, 49152)
    pt_m = shared("pt_m", [P, 2, 2, SEQ], R, 49152 + E_UNITS * FEAT)
    k_m = shared("k_m", [P, 2, 2, TOK], R, 72704)
    v_m = shared("v_m", [P, 2, TT, 2, 2, HD], R, 84992)
    cq_hi, cq_lo = shared("cq_hi", [P, KQ, TOK], R, 0), shared("cq_lo", [P, KQ, TOK], R, KQ * FEAT)
    ckv_hi, ckv_lo = shared("ckv_hi", [P, KKV, TOK], R, 18432), shared("ckv_lo", [P, KKV, TOK], R, 97280)
    e_s = shared("e_s", [P, E_UNITS, 896], F, 49152)
    pt_s = shared("pt_s", [P, 2, 2, SEQ], R, 67072)
    k_s = shared("k_s", [P, KVH, 2, TOK], R, 75264)
    v_s = shared("v_s", [P, TT, 2 * KVH, 2, HD], R, 87552)
    lat_f, lat_sq = shared("lat_f", [P, KKV, TOK], F, 49152), shared("lat_sq", [P, KKV, TOK], F, 55296)
    lat_r = shared("lat_r", [P, TOK], F, 61440)
    cq_sq = shared("cq_sq", [P, KQ, TOK], F, 24576)
    aq_sq_x, aq_sq_c = shared("aq_sq_x", [P, SEQ], F, 72704), shared("aq_sq_c", [P, CTX], F, 99840)
    xres = shared("xres", [P, TT, D], F, 24576)
    gate = shared("gate", [P, 2, D], F, 90112)
    x_add = shared("x_add", [P, 256], F, 98304)
    a_row = shared("a_row", [5, 2, 256], F, 101792)
    xn = shared("xn", [P, 2, D], F, 49152)
    x_mod = shared("x_mod", [P, 2, D], F, 57344)
    fin_w = shared("fin_w", [P, D], F, 60416)
    v_rows = shared("v_rows", [V_ROWS, P], F, 60416)
    mask_f = shared("mask_f", [P, 2 * P], F, 61440)
    x_rows = t_in["x"][0, :, :].rearrange("(t p) d -> p t d", p=P)
    out_rows = out[0, :, :].rearrange("(t p) d -> p t d", p=P)

    small_loads = {
        "const_load": [(ident[:, :], t_in["consts"][:, K_ID:K_ID + P]), (ones[:, :], t_in["consts"][:, K_ONE:K_ONE + P]),
                       (blk[:, :], t_in["consts"][:, K_BLK:K_BLK + P]), (mask_f[:, :], t_in["consts"][:, K_MPREV:K_MPREV + 2 * P]),
                       (sel[:, :], t_in["consts"][0:5, K_SEL:K_SEL + 2])],
        "vec_load": [(v_rows[V_C:V_C + KD, :], t_in["c"][0, :].rearrange("(k p) -> k p", p=P)),
                     (v_rows[V_CC:V_CC + KD, :], t_in["c_ctx"].rearrange("(k p) -> k p", p=P)),
                     (sink_in[:, :], t_in["swa_sink"].rearrange("l h -> (l h)").rearrange("(a n) -> a n", a=1))],
    }
    for l in range(LAYERS):
        r = V_L + l * V_PER
        small_loads["vec_load"] += [
            (v_rows[r + V_NORM:r + V_NORM + KD, :], t_in["norm_w"][l, :].rearrange("(k p) -> k p", p=P)),
            (v_rows[r + V_QN:r + V_QN + KQ, :], t_in["mla_q_norm"][l, :].rearrange("(k p) -> k p", p=P)),
            (v_rows[r + V_KVN:r + V_KVN + KKV, :], t_in["mla_kv_norm"][l, :].rearrange("(k p) -> k p", p=P))]
        for v, name in ((V_AXQ, "ax_q_norm"), (V_AXK, "ax_k_norm")):
            for half in range(2):
                small_loads["vec_load"].append((v_rows[r + v:r + v + 1, half * HD:(half + 1) * HD], t_in[name][l:l + 1, :]))
    CONST_LOADS, VEC_LOADS = len(small_loads["const_load"]), len(small_loads["vec_load"])
    X_LOADS = [4, 5]
    assert max(ends) <= nc.sbuf_usable_end, (max(ends), nc.sbuf_usable_end)

    with ExitStack() as stack:
        def psum(name, cols):
            return stack.enter_context(nc.psum_tensor(name, [P, cols], F))

        acc = [psum("acc0", 512), psum("acc1", 512)]
        wide = [psum("wide0", 1024), psum("wide1", 1024)]
        ptp = [psum("ptp0", 512), psum("ptp1", 512)]

        def semaphore(name):
            return stack.enter_context(nc.semaphore(name))

        const_load, vec_load, tab_load, fin_load = (semaphore(k) for k in ("const_load", "vec_load", "tab_load", "fin_load"))
        x_load, x_saved = semaphore("x_load"), semaphore("x_saved")
        raw_load = [semaphore(f"raw_load{i}") for i in range(RAW_SLOTS)]
        bias_load, out_saved = ([semaphore(f"{k}{i}") for i in range(2)] for k in ("bias_load", "out_saved"))
        vec_done, vec_ready, consts_ready = semaphore("vec_done"), semaphore("vec_ready"), semaphore("consts_ready")
        cs_th, cs_ready, mod_ready = semaphore("cs_th"), semaphore("cs_ready"), semaphore("mod_ready")
        w_hi_ready, w_lo_ready = semaphore("w_hi_ready"), semaphore("w_lo_ready")
        acc_done, ev_a, acc_free = semaphore("acc_done"), semaphore("ev_a"), semaphore("acc_free")
        h_done, l_done = semaphore("h_done"), semaphore("l_done")
        rope_link, rope_done, axt_ready = semaphore("rope_link"), semaphore("rope_done"), semaphore("axt_ready")
        stat_done, th_done = semaphore("stat_done"), semaphore("th_done")
        s_done, max_done, exp_done, norm_done = (semaphore(k) for k in ("s_done", "max_done", "exp_done", "norm_done"))
        pt_done, pt_hi_ready, pt_lo_ready = semaphore("pt_done"), semaphore("pt_hi_ready"), semaphore("pt_lo_ready")
        pv_done, o_copied, o_free = semaphore("pv_done"), semaphore("o_copied"), semaphore("o_free")
        x_sq, x_stat, x_n, x_t = (semaphore(k) for k in ("x_sq", "x_stat", "x_n", "x_t"))
        x_f, x_b, x_h, x_l = (semaphore(k) for k in ("x_f", "x_b", "x_h", "x_l"))
        xr_done, f_ready, chain_v = semaphore("xr_done"), semaphore("f_ready"), semaphore("chain_v")
        block = stack.enter_context(nc.Block())

        def counting():
            seen = {}

            def new(semaphore_, count):
                higher = count > seen.get(id(semaphore_), 0)
                if higher:
                    seen[id(semaphore_)] = count
                return higher
            return new

        def cols(tg):
            return slice(0, CTX) if tg == "c" else slice(CTX, TOK)

        def size(tg):
            return CTX if tg == "c" else SEQ

        def f(ap):
            return ap.bitcast(F)

        def chunk_dma(c):
            kind, l = chunks[c][0], chunks[c][1]
            raw = w_raw[:, c % RAW_SLOTS, :]
            if kind == "win":
                c0, w = chunks[c][2:]
                return [(raw[:, 0:KD * w].rearrange("p (k c) -> p k c", k=KD),
                         t_in["w_in"][l, :, c0:c0 + w].rearrange("(k p) c -> p k c", p=P))]
            if kind == "v":
                half = chunks[c][2]
                rows = slice(half * D // 2, (half + 1) * D // 2)
                dst = raw.rearrange("p (k c) -> p k c", k=KD // 2)
                return [(dst[:, :, i * P:(i + 1) * P], t_in["w_in"][l, rows, c0:c0 + P].rearrange("(k p) c -> p k c", p=P))
                        for i, c0 in enumerate((C_SV, C_AV))]
            if kind in ("ada", "wout"):
                j, half = chunks[c][2:4]
                src = t_in["ada_w" if kind == "ada" else "w_out"]
                return [(raw.rearrange("p (k c) -> p k c", k=KD // 2),
                         src[l, half * D // 2:(half + 1) * D // 2, j * 256:(j + 1) * 256].rearrange("(k p) c -> p k c", p=P))]
            if kind == "uq":
                w, p = 2 * MLA_K, chunks[c][2]
                return [(raw[:, 0:KQ * w].rearrange("p (k c) -> p k c", k=KQ),
                         t_in["mla_w_uq"][l, :, p * w:(p + 1) * w].rearrange("(k p) c -> p k c", p=P))]
            if kind == "ukv":
                w, p = 2 * P, chunks[c][2]
                return [(raw[:, 0:KKV * w].rearrange("p (k c) -> p k c", k=KKV),
                         t_in["mla_w_ukv"][l, :, p * w:(p + 1) * w].rearrange("(k p) c -> p k c", p=P))]
            b, t = chunks[c][2:]
            src = t_in[("w_o_mla", "w_o_swa", "w_o_ax")[b]]
            return [(raw[:, 0:KO * P].rearrange("p (k c) -> p k c", k=KO),
                     src[l, :, t * P:(t + 1) * P].rearrange("(k p) c -> p k c", p=P))]

        def chunk_size(c):
            return {"win": KD * (chunks[c][3] if chunks[c][0] == "win" else 0), "v": CHUNK, "ada": CHUNK, "wout": CHUNK,
                    "uq": KQ * 2 * MLA_K, "ukv": KKV * 2 * P, "wo": KO * P}[chunks[c][0]]

        loads = [0] * len(chunks)
        for c in range(len(chunks)):
            loads[c] = (loads[c - RAW_SLOTS] if c >= RAW_SLOTS else 0) + 16 * len(chunk_dma(c))

        @block.sync
        def _(sp):
            new = counting()
            for c in range(len(chunks)):
                if c >= RAW_SLOTS:
                    if new(w_lo_ready, c - RAW_SLOTS + 1):
                        sp.wait_ge(w_lo_ready, c - RAW_SLOTS + 1)
                for dst, src in chunk_dma(c):
                    sp.dma_start(dst, src).then_inc(raw_load[c % RAW_SLOTS], 16)
                if chunks[c][0] == "ada" and chunks[c][3] == 0:
                    l, j, _, slot, reader = chunks[c][1:]
                    if reader:
                        if new(acc_done, reader):
                            sp.wait_ge(acc_done, reader)
                    sp.dma_start(a_row[4:5, slot, :], t_in["ada_b"][l:l + 1, j * 256:(j + 1) * 256]).then_inc(bias_load[slot], 16)
            for i in range(TT - TT_CTX):
                if new(f_ready, i + 1):
                    sp.wait_ge(f_ready, i + 1)
                sp.dma_start(out_rows[:, i, :], xn[:, i % 2, :]).then_inc(out_saved[i % 2], 16)
            for i in range(2):
                if new(out_saved[i], 16 * (TT - TT_CTX) // 2):
                    sp.wait_ge(out_saved[i], 16 * (TT - TT_CTX) // 2)

        def q_of(u):
            cs_ = slice(u["tt"] * P, (u["tt"] + 1) * P)
            if u["branch"] == "mla":
                return [q_m[0:MLA_K, u["h"] % 2, i, cs_] for i in range(2)]
            return [q_s[:, u["h"] % 4, cs_]]

        def k_of(u, k0, nk):
            if u["branch"] == "mla":
                return [k_m[0:MLA_K, u["h"] % 2, i, k0:k0 + nk] for i in range(2)]
            return [k_s[:, u["h"] // (HEADS // KVH), i, k0:k0 + nk] for i in range(2)]

        def v_of(pa, kt):
            if pa["branch"] == "mla":
                v = v_m[:, (pa["h"] // 2) % 2, kt, pa["h"] % 2, :, :]
            else:
                v = v_s[:, kt, (KVH if pa["branch"] == "ax" else 0) + pa["h"] // (HEADS // KVH), :, :]
            return v.rearrange("p a d -> p (a d)")

        def e_of(u, c0=0, c1=None):
            e = e_m if u["branch"] != "swa" else e_s
            return e[:, u["slot"], c0:(u["width"] if c1 is None else c1)]

        def pt_of(t, part):
            p = pt_m if t["pa"]["branch"] != "swa" else pt_s
            return p[:, t["n"] % 2, part, 0:t["width"]]

        def o_tokens(pa):
            return slice(pa["units"][0]["tt"] * P, (pa["units"][-1]["tt"] + 1) * P)

        def o_rows(pa):
            return (slice(0, HD), slice(HD, P)) if pa["h"] % 2 == 0 else (slice(HD, P), slice(0, HD))

        def matmuls(g):
            a = acc[g["bank"]]
            out_ = []

            def run(dst, pairs):
                for i, (lhs, rhs) in enumerate(pairs):
                    out_.append((dst, lhs, rhs, i == 0, i == len(pairs) - 1))

            def split3(lh, ll, rh, rl):
                return [(lh, rh), (lh, rl), (ll, rh)]

            mode = g["mode"]
            if mode == "w":
                s = g["chunks"][0] % SPLIT_SLOTS
                hi, lo = {"h": (h_hi, h_lo), "cq": (cq_hi, cq_lo), "ckv": (ckv_hi, ckv_lo), "og": (og_hi, og_lo)}[g["src"]]
                pairs = []
                for k in range(g["k"]):
                    c0 = k * g["width"] + g["co"]
                    w = slice(c0, c0 + g["m"])
                    pairs += [(w_hi[:, s, w], hi[:, k, cols(g["tg"])]), (w_hi[:, s, w], lo[:, k, cols(g["tg"])]),
                              (w_lo[:, s, w], hi[:, k, cols(g["tg"])])]
                run(a[0:g["m"], 0:size(g["tg"])], pairs)
            elif mode in ("vs", "wout", "ada"):
                hi, lo = (h_hi, h_lo) if mode == "vs" else (y_hi, y_lo)
                for i, tt in enumerate(g.get("tts", [g.get("tt")])):
                    pairs = []
                    for k in range(KD):
                        s = g["chunks"][k // (KD // 2)] % SPLIT_SLOTS
                        w = slice((k % (KD // 2)) * 256, (k % (KD // 2) + 1) * 256)
                        if mode == "ada":
                            pairs += [(cs[:, k, :], w_hi[:, s, w]), (cs[:, k, :], w_lo[:, s, w])]
                        else:
                            ts = slice(tt * P, (tt + 1) * P)
                            pairs += split3(hi[:, k, ts], lo[:, k, ts], w_hi[:, s, w], w_lo[:, s, w])
                    run(a[0:4 if mode == "ada" else P, i * 256:(i + 1) * 256], pairs)
            elif mode == "vm":
                s = g["chunks"][0] % SPLIT_SLOTS
                for i, tt in enumerate(g["tts"]):
                    pairs = []
                    for k in range(KKV):
                        wv = [w[:, s, k * 256:(k + 1) * 256].rearrange("p (h a d) -> p h a d", h=2, a=2)[:, :, 1, :] for w in (w_hi, w_lo)]
                        ts = slice(tt * P, (tt + 1) * P)
                        pairs += split3(ckv_hi[:, k, ts], ckv_lo[:, k, ts], *wv)
                    run(a[:, i * 2 * HD:(i + 1) * 2 * HD], pairs)
            elif mode == "statb":
                m = ones if g["what"] == "ckv" else blk
                run(a[:, 0:size(g["tg"])], [(m[:, :], lat_sq[:, t, cols(g["tg"])]) for t in range(g["tiles"])])
            elif mode == "statq":
                for tt in g["tts"]:
                    ts = slice(tt * P, (tt + 1) * P)
                    if g["what"] == "mla":
                        run(a[:, 2 * tt:2 * tt + 2], [(cq_sq[:, t, ts], ones[:, 0:2]) for t in range(KQ)])
                    else:
                        sq = aq_sq_c[:, ts] if tt < TT_CTX else aq_sq_x[:, (tt - TT_CTX) * P:(tt - TT_CTX + 1) * P]
                        run(a[:, 2 * tt:2 * tt + 2], [(sq, blk[:, 0:P:HD])])
            elif mode == "adaT":
                for i in range(2):
                    run(a[:, 2 * i:2 * i + 2], [(a_row[0:5, g["slot"], i * P:(i + 1) * P], sel[0:5, :])])
            elif mode == "adaG":
                run(a[:, 0:256], [(sel[0:5, g["s"]:g["s"] + 1].to_broadcast([5, P]), a_row[0:5, g["slot"], :])])
            return out_

        @block.tensor
        def _(pe):
            new = counting()
            if new(const_load, 16 * CONST_LOADS):
                pe.wait_ge(const_load, 16 * CONST_LOADS)
            if new(vec_load, 16 * VEC_LOADS):
                pe.wait_ge(vec_load, 16 * VEC_LOADS)
            nc.tensor.transpose(acc[0][:, 0:V_ROWS], v_rows[:, :], ident[0:V_ROWS, 0:V_ROWS]).then_inc(vec_done, 1)
            if new(vec_ready, 1):
                pe.wait_ge(vec_ready, 1)
            if new(consts_ready, 1):
                pe.wait_ge(consts_ready, 1)
            for e in events:
                ev = e["ev"]
                if ev == "G":
                    g, part, mode = e["g"], e["part"], e["g"]["mode"]
                    if part == 0:
                        need = g["needs"]
                        if mode == "vs" or (mode == "w" and g["src"] == "h"):
                            if new(x_l, need["x_l"]):
                                pe.wait_ge(x_l, need["x_l"])
                        elif mode == "vm" or (mode == "w" and g["src"] != "og"):
                            if new(acc_free, need["acc_free"]):
                                pe.wait_ge(acc_free, need["acc_free"])
                            if new(l_done, need["l_done"]):
                                pe.wait_ge(l_done, need["l_done"])
                        elif mode in ("w", "wout"):
                            if new(l_done, need["l_done"]):
                                pe.wait_ge(l_done, need["l_done"])
                        elif mode in ("statb", "statq"):
                            if new(ev_a, need["ev_a"]):
                                pe.wait_ge(ev_a, need["ev_a"])
                        elif mode == "ada":
                            if new(cs_ready, 1):
                                pe.wait_ge(cs_ready, 1)
                        else:
                            if new(acc_free, need["acc_free"]):
                                pe.wait_ge(acc_free, need["acc_free"])
                            if new(bias_load[g["slot"]], 16 * need["loads"]):
                                pe.wait_ge(bias_load[g["slot"]], 16 * need["loads"])
                        if g["chunks"]:
                            if new(w_lo_ready, g["chunks"][-1] + 1):
                                pe.wait_ge(w_lo_ready, g["chunks"][-1] + 1)
                        before = g["before"]
                        if before is not None and before["dve"]:
                            if new(acc_free, before["v"]):
                                pe.wait_ge(acc_free, before["v"])
                        elif before is not None:
                            if new(ev_a, before["a"]):
                                pe.wait_ge(ev_a, before["a"])
                        if g["bank"] == 1:
                            if new(o_free, g["passes"]):
                                pe.wait_ge(o_free, g["passes"])
                    mm = matmuls(g)
                    a, b = part * len(mm) // g["parts"], (part + 1) * len(mm) // g["parts"]
                    for dst, lhs, rhs, first, last in mm[a:b]:
                        ins = nc.tensor.matmul(dst, lhs, rhs, start=first, stop=last)
                    if part == g["parts"] - 1:
                        ins.then_inc(acc_done, 1)
                elif ev == "S":
                    u = e["u"]
                    if new(acc_free, u["ready_free"]):
                        pe.wait_ge(acc_free, u["ready_free"])
                    if new(l_done, u["ready_l"]):
                        pe.wait_ge(l_done, u["ready_l"])
                    if u["n"] >= 2:
                        if new(exp_done, u["n"] - 1):
                            pe.wait_ge(exp_done, u["n"] - 1)
                    if new(x_f, u["x"]):
                        pe.wait_ge(x_f, u["x"])
                    w = wide[u["n"] % 2]
                    if u["branch"] == "swa":
                        i = u["l"] * HEADS + u["h"]
                        nc.tensor.matmul(w[:, u["lo"]:u["lo"] + 2], ones[0:1, :], sink[0:1, i, :], start=True, stop=True)
                    for c0, k0, nk in u["pieces"]:
                        qs, ks = q_of(u), k_of(u, k0, nk)
                        pairs = [(qs[0], ks[0]), (qs[0], ks[1])] + ([(qs[1], ks[0])] if len(qs) == 2 else [])
                        masks = [m for m in u["masks"] if c0 <= m[0] < c0 + nk]
                        for i, (lhs, rhs) in enumerate(pairs):
                            ins = nc.tensor.matmul(w[:, c0:c0 + nk], lhs, rhs, start=(i == 0), stop=(i == len(pairs) - 1 and not masks))
                        for i, (m0, which) in enumerate(masks):
                            ins = nc.tensor.matmul(w[:, m0:m0 + P], ident_r[:, :], mask_r[:, which, :], start=False, stop=(i == len(masks) - 1))
                    ins.then_inc(s_done, 1)
                elif ev == "T":
                    t = e["t"]
                    if new(norm_done, t["pa"]["units"][-1]["n"] + 1):
                        pe.wait_ge(norm_done, t["pa"]["units"][-1]["n"] + 1)
                    if t["n"] >= 2:
                        if new(pt_lo_ready, t["n"] - 1):
                            pe.wait_ge(pt_lo_ready, t["n"] - 1)
                    for kt, q0, q1, block0 in t["blocks"]:
                        for i in range(q0, q1):
                            u, b = t["pa"]["units"][i], (block0 + i - q0) * P
                            c0 = u["kts"][kt]
                            ins = nc.tensor.transpose(ptp[t["n"] % 2][:, b:b + P], e_of(u, c0, c0 + P), ident[:, :])
                    ins.then_inc(pt_done, 1)
                elif ev == "PV":
                    t, pa = e["t"], e["t"]["pa"]
                    if new(pt_lo_ready, t["n"] + 1):
                        pe.wait_ge(pt_lo_ready, t["n"] + 1)
                    if new(acc_free, t["values"]):
                        pe.wait_ge(acc_free, t["values"])
                    if t["first"]:
                        if new(o_free, pa["o"]):
                            pe.wait_ge(o_free, pa["o"])
                        before = t["bank1"]
                        if before is not None and before["dve"]:
                            if new(acc_free, before["v"]):
                                pe.wait_ge(acc_free, before["v"])
                        elif before is not None:
                            if new(ev_a, before["a"]):
                                pe.wait_ge(ev_a, before["a"])
                    for i, (kt, q0, q1, block0) in enumerate(t["blocks"]):
                        dst, b = acc[1][:, q0 * P:q1 * P], slice(block0 * P, (block0 + q1 - q0) * P)
                        nc.tensor.matmul(dst, v_of(pa, kt), pt_of(t, 0)[:, b], start=t["first"] and i == 0, stop=False)
                        ins = nc.tensor.matmul(dst, v_of(pa, kt), pt_of(t, 1)[:, b], start=False, stop=t["last"] and i == len(t["blocks"]) - 1)
                    ins.then_inc(pv_done, 1)
                elif ev == "XN":
                    tt, i = e["tt"], e["n"]
                    if new(x_n, i + 1):
                        pe.wait_ge(x_n, i + 1)
                    if new(exp_done, e["s"]):
                        pe.wait_ge(exp_done, e["s"])
                    if i >= 2:
                        if new(x_f, i - 1):
                            pe.wait_ge(x_f, i - 1)
                    for k in range(KD):
                        ins = nc.tensor.transpose(wide[i % 2][:, k * P:(k + 1) * P], xn[:, i % 2, k * P:(k + 1) * P], ident[:, :])
                    ins.then_inc(x_t, 1)

        def pieces(g):
            tg, what, l = g.get("tg"), g["what"], g["l"]
            c = cols(tg) if tg else None
            v0 = V_L + l * V_PER
            src = acc[g["bank"]]
            N = size(tg) if tg else None
            if g.get("roped"):
                src = rot
            if what == "cq":
                return [(cq_hi[:, g["t"], c], cq_lo[:, g["t"], c], src[:, 0:N])], vec[:, v0 + V_QN + g["t"]:v0 + V_QN + g["t"] + 1]
            if what == "qm":
                s = g["head"] % 2
                return [(q_m[0:MLA_K, s, 0, c], q_m[0:MLA_K, s, 1, c], src[0:MLA_K, 0:N])], None
            if what == "km":
                s = g["head"] % 2
                return [(k_m[0:MLA_NOPE, s, 0, c], k_m[0:MLA_NOPE, s, 1, c], src[0:MLA_NOPE, 0:N])], None
            if what == "kr":
                rows = slice(MLA_NOPE, MLA_K)
                s = src[rows, 0:N] if g["roped"] else src[0:MLA_ROPE, 0:N]
                return [(k_m[rows, i, 0, c], k_m[rows, i, 1, c], s) for i in range(2)], None
            if what in ("k", "ak"):
                if what == "ak":
                    src, N0 = lat_f[:, 0, :], c
                else:
                    N0 = slice(0, N)
                out_ = []
                for kv in range(KVH):
                    rows = slice(kv * HD, (kv + 1) * HD)
                    for half in range(2):
                        d = slice(half * HD, (half + 1) * HD)
                        out_.append((k_s[d, kv, 0, c], k_s[d, kv, 1, c], src[rows, N0], k_s[rows, kv, 0, c]))
                return out_, None
            if what == "ckv":
                return [(ckv_hi[:, :, c], ckv_lo[:, :, c], lat_f[:, :, c])], None
            if what == "qs":
                s = g["head"] % 4
                up, dn = slice(0, HD), slice(HD, P)
                w = None
                if g["branch"] == "ax" and not g["roped"]:
                    w = vec[:, v0 + V_AXQ:v0 + V_AXQ + 1]
                return [(q_s[up, s, c], q_s[dn, s, c], src[up, 0:N]), (q_s[dn, s + 1, c], q_s[up, s + 1, c], src[dn, 0:N])], w
            if what in ("vs", "vm"):
                t0, t1 = g["tts"][0], g["tts"][-1] + 1
                heads = 2 * KVH if what == "vs" else 2
                v = v_s[:, t0:t1] if what == "vs" else v_m[:, g["pair"] % 2, t0:t1]
                got = src[:, 0:(t1 - t0) * heads * HD].rearrange("p (t g d) -> p t g d", g=heads, d=HD)
                return [(v[:, :, :, 0, :], v[:, :, :, 1, :], got)], None
            raise KeyError(what)

        def rows_of(ap, w):
            s = ap.start_partition if not callable(ap.start_partition) else ap.start_partition()
            return w[s:s + ap.shape[0], :]

        def high_parts(ps, w):
            for p in ps:
                if w is None:
                    ins = nc.scalar.activation(p[0], p[2], ACT.Copy)
                else:
                    ins = nc.scalar.activation(p[0], p[2], ACT.Identity, scale=rows_of(p[2], w))
            return ins

        def low_parts(ps, w):
            for p in ps:
                hi = p[3] if len(p) == 4 else p[0]
                if w is None:
                    ins = nc.vector.tensor_tensor(p[1], p[2], f(hi), ALU.subtract)
                else:
                    ins = nc.vector.scalar_tensor_tensor(p[1], p[2], rows_of(p[2], w), f(hi), ALU.mult, ALU.subtract)
            return ins

        DIRECT = ("cq", "qm", "km", "kr", "ks", "qs", "vs", "vm")

        def squares_of(g):
            c = cols(g["tg"]) if "tg" in g else None
            if g["kind"] == "cq":
                return cq_sq[:, g["t"], c]
            if g["kind"] in ("ckv", "ak"):
                return lat_sq[:, g.get("t", 0), c]
            if g["kind"] == "qs" and g["branch"] == "ax":
                return (aq_sq_c if g["tg"] == "c" else aq_sq_x)[:, :]
            return None

        @block.scalar
        def _(act):
            new = counting()
            for dst, src in small_loads["const_load"]:
                act.dma_start(dst, src).then_inc(const_load, 16)
            for dst, src in small_loads["vec_load"]:
                act.dma_start(dst, src).then_inc(vec_load, 16)
            if new(const_load, 16 * CONST_LOADS):
                act.wait_ge(const_load, 16 * CONST_LOADS)
            nc.scalar.activation(ident_r[:, :], ident[:, :], ACT.Copy)
            nc.scalar.activation(mask_r[:, :, :], mask_f[:, :].rearrange("p (a b) -> p a b", a=2), ACT.Copy).then_inc(consts_ready, 1)
            if new(vec_ready, 1):
                act.wait_ge(vec_ready, 1)
            nc.scalar.activation(cs_f[:, 0, :], vec[:, 0:2 * KD], ACT.Tanh, scale=0.5).then_inc(cs_th, 1)
            tabs = xl = 0
            for e in events:
                ev = e["ev"]
                if ev == "W" and e["c"] < len(chunks):
                    c = e["c"]
                    if new(raw_load[c % RAW_SLOTS], loads[c]):
                        act.wait_ge(raw_load[c % RAW_SLOTS], loads[c])
                    if new(acc_done, e["reuse"]):
                        act.wait_ge(acc_done, e["reuse"])
                    k = chunk_size(c)
                    nc.scalar.activation(w_hi[:, c % SPLIT_SLOTS, 0:k], w_raw[:, c % RAW_SLOTS, 0:k], ACT.Copy).then_inc(w_hi_ready, 1)
                elif ev == "E" and e["g"]["act"]:
                    g = e["g"]
                    kind, src = g["kind"], acc[g["bank"]]
                    N = size(g["tg"]) if "tg" in g else None
                    if new(acc_done, g["n"] + 1):
                        act.wait_ge(acc_done, g["n"] + 1)
                    sq = squares_of(g)
                    ins = None
                    if sq is not None:
                        ins = nc.scalar.activation(sq, src[:, 0:N], ACT.Square)
                    if kind in DIRECT and not g.get("roped"):
                        ins = high_parts(*pieces(g))
                    elif kind == "statb":
                        if new(stat_done, g["stat"] - 1):
                            act.wait_ge(stat_done, g["stat"] - 1)
                        ins = nc.scalar.activation(lat_r[:, cols(g["tg"])], src[:, 0:N], ACT.Sqrt, scale=1.0 / g["nsum"], bias=eps_col[:, 0:1])
                    elif kind == "statq":
                        t0, t1 = g["tts"][0], g["tts"][-1] + 1
                        got = src[:, 2 * t0:2 * t1].rearrange("p (t a) -> p a t", a=2)
                        if g["what"] == "mla":
                            dst, got, count, col = rq[:, 0, t0:t1], got[:, 0, :], Q_RANK, 1
                        else:
                            dst, count, col = rq[:, g["head"]:g["head"] + 2, t0:t1], HD, 2
                        s2 = SCALE[g["what"]] ** 2
                        ins = nc.scalar.activation(dst, got, ACT.Sqrt, scale=1.0 / (count * s2), bias=eps_col[:, col:col + 1])
                    elif kind in ("z", "g"):
                        before = g["th_before"]
                        if before is not None and "th" in before:
                            if new(th_done, before["th"]):
                                act.wait_ge(th_done, before["th"])
                        elif before is not None:
                            if new(acc_free, before["v"]):
                                act.wait_ge(acc_free, before["v"])
                        ins = nc.scalar.activation(th[:, g["th_slot"], 0:N], src[:, 0:N], ACT.Tanh, scale=0.5)
                    ins.then_inc(ev_a, 1)
                elif ev == "H":
                    g = e["g"]
                    if g["kind"] == "statb":
                        if new(stat_done, g["stat"]):
                            act.wait_ge(stat_done, g["stat"])
                        ins = high_parts(*pieces(g))
                    elif g["kind"] == "z":
                        if new(th_done, g["th"]):
                            act.wait_ge(th_done, g["th"])
                        ins = nc.scalar.activation(og_hi[:, g["t"], cols(g["tg"])], o_t[:, g["t"], cols(g["tg"])], ACT.Copy)
                    elif g["kind"] == "y":
                        if new(th_done, g["th"]):
                            act.wait_ge(th_done, g["th"])
                        ins = nc.scalar.activation(y_hi[:, g["t"], cols(g["tg"])], y2[:, g["t"], cols(g["tg"])], ACT.Copy, scale=0.5)
                    else:
                        if new(rope_done, g["rope"]):
                            act.wait_ge(rope_done, g["rope"])
                        ins = high_parts(*pieces(g))
                    ins.then_inc(h_done, 1)
                elif ev == "M":
                    u = e["u"]
                    if new(max_done, u["n"] + 1):
                        act.wait_ge(max_done, u["n"] + 1)
                    if new(pt_done, u["e_free"]):
                        act.wait_ge(pt_done, u["e_free"])
                    r = u["n"] % 8
                    if u["branch"] == "swa":
                        scale = SCALE["swa"]
                    else:
                        i = 0 if u["branch"] == "mla" else u["h"]
                        scale = rq[:, i, u["tt"]:u["tt"] + 1]
                    nc.scalar.activation(e_of(u), wide[u["n"] % 2][:, u["lo"]:u["lo"] + u["width"]], ACT.Exp,
                                         bias=nbias[:, r:r + 1], scale=scale, accum_out=esum[:, r:r + 1]).then_inc(exp_done, 1)
                elif ev == "T":
                    t = e["t"]
                    if new(pt_done, t["n"] + 1):
                        act.wait_ge(pt_done, t["n"] + 1)
                    if t["n"] >= 2:
                        if new(pv_done, t["n"] - 1):
                            act.wait_ge(pv_done, t["n"] - 1)
                    nc.scalar.activation(pt_of(t, 0), ptp[t["n"] % 2][:, 0:t["width"]], ACT.Copy).then_inc(pt_hi_ready, 1)
                elif ev == "O":
                    pa = e["pa"]
                    own, other = o_rows(pa)
                    if new(pv_done, pa["pt_end"]):
                        act.wait_ge(pv_done, pa["pt_end"])
                    if new(o_free, pa["o"]):
                        act.wait_ge(o_free, pa["o"])
                    k = len(pa["units"]) * P
                    nc.scalar.activation(o_half[own, 0:k], acc[1][other, 0:k], ACT.Copy).then_inc(o_copied, 1)
                elif ev == "XL":
                    if new(acc_done, e["acc"]):
                        act.wait_ge(acc_done, e["acc"])
                    if new(l_done, e["l_done"]):
                        act.wait_ge(l_done, e["l_done"])
                    if e["tail"] and e["l"] > 0:
                        if new(x_saved, 16):
                            act.wait_ge(x_saved, 16)
                    if e["l"] == 0:
                        act.dma_start(xres[:, 0:TT_CTX, :], t_in["ctx"][0, :, :].rearrange("(t p) d -> p t d", p=P)).then_inc(x_load, 16)
                        act.dma_start(xres[:, TT_CTX:TT, :], x_rows).then_inc(x_load, 16)
                    else:
                        act.dma_start(xres[:, TT_CTX:TT, :], x_mid.rearrange("(t p) d -> p t d", p=P)).then_inc(x_load, 16)
                        act.dma_start(fin_w[:, :], t_in["final_norm_w"].rearrange("(a d) -> a d", a=1).to_broadcast([P, D])).then_inc(fin_load, 16)
                    xl += 1
                elif ev == "TAB":
                    if new(acc_free, e["free"]):
                        act.wait_ge(acc_free, e["free"])
                    if new(rope_done, e["rope"]):
                        act.wait_ge(rope_done, e["rope"])
                    a, b = ("cos_m", "sin_m") if e["which"] == "m" else ("cos_s", "sin_s")
                    act.dma_start(cos[:, :], t_in[a]).then_inc(tab_load, 16)
                    act.dma_start(sin[:, :], t_in[b]).then_inc(tab_load, 16)
                elif ev in ("XN", "FN"):
                    tt = e["tt"]
                    if ev == "XN" and e["l"] == 0:
                        if new(x_load, 32):
                            act.wait_ge(x_load, 32)
                    else:
                        if new(xr_done, e["xr"]):
                            act.wait_ge(xr_done, e["xr"])
                    i = e["n"] + (LAYERS * TT if ev == "FN" else 0)
                    if ev == "XN":
                        if i >= 2:
                            if new(x_t, i - 1):
                                act.wait_ge(x_t, i - 1)
                    else:
                        if new(x_t, LAYERS * TT):
                            act.wait_ge(x_t, LAYERS * TT)
                        if e["n"] >= 2:
                            if new(out_saved[i % 2], 16 * (e["n"] // 2)):
                                act.wait_ge(out_saved[i % 2], 16 * (e["n"] // 2))
                    nc.scalar.activation(xn[:, i % 2, :], xres[:, tt, :], ACT.Square, accum_out=ssq[:, tt:tt + 1]).then_inc(x_sq, 1)
                    if new(x_sq, i + 1):
                        act.wait_ge(x_sq, i + 1)
                    nc.scalar.activation(rstd[:, tt:tt + 1], ssq[:, tt:tt + 1], ACT.Sqrt, scale=1.0 / D, bias=eps_col[:, 0:1]).then_inc(x_stat, 1)
                elif ev == "XM":
                    tt, i = e["tt"], e["n"]
                    if new(x_b, i + 1):
                        act.wait_ge(x_b, i + 1)
                    m = x_mod[:, i % 2, :].rearrange("p (k t) -> p k t", k=KD)
                    nc.scalar.activation(h_hi[:, :, tt * P:(tt + 1) * P], m, ACT.Copy).then_inc(x_h, 1)
                elif ev == "XS":
                    if new(xr_done, e["xr"]):
                        act.wait_ge(xr_done, e["xr"])
                    act.dma_start(x_mid.rearrange("(t p) d -> p t d", p=P), xres[:, TT_CTX:TT, :]).then_inc(x_saved, 16)
            for i in range(2):
                if new(out_saved[i], 16 * (TT - TT_CTX) // 2):
                    act.wait_ge(out_saved[i], 16 * (TT - TT_CTX) // 2)
            if new(x_saved, 16):
                act.wait_ge(x_saved, 16)

        @block.gpsimd
        def _(pool):
            new = counting()
            link = splits = tiles = 0
            for e in events:
                ev = e["ev"]
                if ev == "W" and e["c"] < len(chunks):
                    c = e["c"]
                    splits = c + 1
                    k = chunk_size(c)
                    if new(w_hi_ready, c + 1):
                        pool.wait_ge(w_hi_ready, c + 1)
                    nc.gpsimd.tensor_tensor(w_lo[:, c % SPLIT_SLOTS, 0:k], w_raw[:, c % RAW_SLOTS, 0:k],
                                            f(w_hi[:, c % SPLIT_SLOTS, 0:k]), ALU.subtract).then_inc(w_lo_ready, 1)
                elif ev == "E" and e["g"].get("roped"):
                    g = e["g"]
                    if new(acc_free, g["v"]):
                        pool.wait_ge(acc_free, g["v"])
                    if new(tab_load, 32 * g["tab"]):
                        pool.wait_ge(tab_load, 32 * g["tab"])
                    if new(axt_ready, g["axt"]):
                        pool.wait_ge(axt_ready, g["axt"])
                    rows = slice(0, g["m"]) if g["kind"] != "kr" else slice(MLA_NOPE, MLA_K)
                    dst = lat_f[rows, 0, cols("x")] if g["kind"] == "ak" else rot[rows, :]
                    if g["kind"] == "kr":
                        if new(w_lo_ready, splits):
                            pool.wait_ge(w_lo_ready, splits)
                        if new(rope_done, g["rope"] - 1):
                            pool.wait_ge(rope_done, g["rope"] - 1)
                        if new(x_l, tiles):
                            pool.wait_ge(x_l, tiles)
                    link += 1
                    nc.gpsimd.tensor_tensor(swapped[rows, :], swapped[rows, :], sin[rows, :], ALU.mult).then_inc(rope_link, 1)
                    if new(rope_link, link):
                        pool.wait_ge(rope_link, link)
                    nc.gpsimd.tensor_tensor(dst, dst, swapped[rows, :], ALU.add).then_inc(rope_done, 1)
                    if g["kind"] == "kr":
                        if new(rope_done, g["rope"]):
                            pool.wait_ge(rope_done, g["rope"])
                elif ev == "XM":
                    tt = e["tt"]
                    if new(x_h, e["n"] + 1):
                        pool.wait_ge(x_h, e["n"] + 1)
                    ts = slice(tt * P, (tt + 1) * P)
                    nc.gpsimd.tensor_tensor(h_lo[:, :, ts], x_mod[:, e["n"] % 2, :].rearrange("p (k t) -> p k t", k=KD), f(h_hi[:, :, ts]), ALU.subtract).then_inc(x_l, 1)
                    tiles += 1

        @block.vector
        def _(dve):
            new = counting()
            chain = [0]

            def link(ins):
                chain[0] += 1
                ins.then_inc(chain_v, 1)
                if new(chain_v, chain[0]):
                    dve.wait_ge(chain_v, chain[0])

            link(nc.vector.memset(eps_col[:, 0:1], EPS))
            link(nc.vector.memset(eps_col[:, 1:2], EPS / SCALE["mla"] ** 2))
            link(nc.vector.memset(eps_col[:, 2:3], EPS / SCALE["ax"] ** 2))
            if new(vec_done, 1):
                dve.wait_ge(vec_done, 1)
            link(nc.vector.tensor_copy(vec[:, :], acc[0][:, 0:V_ROWS]))
            link(nc.vector.stream_shuffle(vec_sw[:, :], vec[:, :], [i ^ 16 for i in range(32)]))
            if new(vec_load, 16 * VEC_LOADS):
                dve.wait_ge(vec_load, 16 * VEC_LOADS)
            link(nc.vector.memset(sink[:, :, 1], NEG))
            nc.vector.tensor_scalar(sink[:, :, 0], sink_in[:, :], 1.0 / SCALE["swa"], None, ALU.mult).then_inc(vec_ready, 1)
            if new(cs_th, 1):
                dve.wait_ge(cs_th, 1)
            link(nc.vector.scalar_tensor_tensor(cs_f[:, 1, :], cs_f[:, 0, :], 1.0, vec[:, 0:2 * KD], ALU.add, ALU.mult))
            link(nc.vector.tensor_scalar(cs_f[:, 0, :], cs_f[:, 1, :], 0.5, None, ALU.mult))
            silu = cs_f[:, 0, :].rearrange("p (s k) -> p k s", s=2)
            link(nc.vector.tensor_copy(cs[:, :, 0:2], silu))
            nc.vector.tensor_tensor(cs[:, :, 2:4], silu, f(cs[:, :, 0:2]), ALU.subtract).then_inc(cs_ready, 1)
            for e in events:
                ev = e["ev"]
                if ev == "E" and e["g"]["dve"]:
                    g = e["g"]
                    kind, src = g["kind"], acc[g["bank"]]
                    tg = g.get("tg")
                    N = size(tg) if tg else None
                    if new(acc_done, g["n"] + 1):
                        dve.wait_ge(acc_done, g["n"] + 1)
                    if g["act"]:
                        if new(ev_a, g["a"]):
                            dve.wait_ge(ev_a, g["a"])
                    if g.get("roped"):
                        if new(rope_done, g["rope_prev"][0]):
                            dve.wait_ge(rope_done, g["rope_prev"][0])
                        if new(l_done, g["rope_prev"][1]):
                            dve.wait_ge(l_done, g["rope_prev"][1])
                        if new(tab_load, 32 * g["tab"]):
                            dve.wait_ge(tab_load, 32 * g["tab"])
                        if new(axt_ready, g["axt"]):
                            dve.wait_ge(axt_ready, g["axt"])
                        pr = slice(0, g["m"])
                        rows = pr if kind != "kr" else slice(MLA_NOPE, MLA_K)
                        flip = 8 if kind in ("kr", "qm") else 16
                        dst = lat_f[rows, 0, cols("x")] if kind == "ak" else rot[rows, :]
                        nc.vector.stream_shuffle(swapped[rows, :], src[pr, 0:N], [i ^ flip for i in range(32)])
                        nc.vector.tensor_tensor(dst, src[pr, 0:N], cos[rows, :], ALU.mult).then_inc(acc_free, 1)
                    elif kind in DIRECT:
                        low_parts(*pieces(g)).then_inc(acc_free, 1)
                    elif kind == "ckv":
                        nc.vector.tensor_copy(lat_f[:, g["t"], cols(tg)], src[:, 0:N]).then_inc(acc_free, 1)
                    elif kind == "ak":
                        i = V_L + g["l"] * V_PER + V_AXK
                        nc.vector.tensor_scalar(lat_f[:, 0, cols(tg)], src[:, 0:N], vec[:, i:i + 1], None, ALU.mult).then_inc(acc_free, 1)
                    elif kind == "statb":
                        r = lat_r[:, cols(tg)]
                        nc.vector.reciprocal(r, r).then_inc(acc_free, 1)
                        if new(acc_free, g["v"]):
                            dve.wait_ge(acc_free, g["v"])
                        if g["what"] == "ak":
                            if new(rope_done, g["rope_done"]):
                                dve.wait_ge(rope_done, g["rope_done"])
                            x = lat_f[:, 0, cols(tg)]
                            ins = nc.vector.tensor_tensor(x, x, r, ALU.mult)
                        else:
                            i = V_L + g["l"] * V_PER + V_KVN
                            for t in range(KKV):
                                x = lat_f[:, t, cols(tg)]
                                ins = nc.vector.scalar_tensor_tensor(x, x, vec[:, i + t:i + t + 1], r, ALU.mult, ALU.mult)
                        ins.then_inc(stat_done, 1)
                    elif kind == "statq":
                        t0, t1 = g["tts"][0], g["tts"][-1] + 1
                        r = rq[:, 0, t0:t1] if g["what"] == "mla" else rq[:, g["head"]:g["head"] + 2, t0:t1]
                        nc.vector.reciprocal(r, r).then_inc(acc_free, 1)
                    elif kind == "z":
                        if new(o_free, g["o_done"]):
                            dve.wait_ge(o_free, g["o_done"])
                        t = th[:, g["th_slot"], 0:N]
                        o = o_t[:, g["t"], cols(tg)]
                        nc.vector.scalar_tensor_tensor(t, t, 1.0, src[:, 0:N], ALU.add, ALU.mult).then_inc(acc_free, 1)
                        if new(acc_free, g["v"]):
                            dve.wait_ge(acc_free, g["v"])
                        nc.vector.scalar_tensor_tensor(o, t, 0.5, o, ALU.mult, ALU.mult).then_inc(th_done, 1)
                    elif kind == "y":
                        if new(ev_a, g["of"]["a"]):
                            dve.wait_ge(ev_a, g["of"]["a"])
                        t = th[:, g["of"]["th_slot"], 0:N]
                        y = y2[:, g["t"], cols(tg)]
                        if g["branch"] == BRANCHES[0]:
                            nc.vector.scalar_tensor_tensor(y, t, 1.0, src[:, 0:N], ALU.add, ALU.mult).then_inc(acc_free, 1)
                        else:
                            nc.vector.scalar_tensor_tensor(t, t, 1.0, src[:, 0:N], ALU.add, ALU.mult).then_inc(acc_free, 1)
                            if new(acc_free, g["v"]):
                                dve.wait_ge(acc_free, g["v"])
                            nc.vector.tensor_tensor(y, y, t, ALU.add).then_inc(th_done, 1)
                    elif kind == "ada":
                        nc.vector.tensor_copy(a_row[0:4, g["slot"], :], src[0:4, 0:256]).then_inc(acc_free, 1)
                    elif kind == "adaT":
                        nc.vector.tensor_copy(mod_col[:, 2 * g["j"]:2 * g["j"] + 2, :],
                                              src[:, 0:4].rearrange("p (b s) -> p b s", b=2)).then_inc(acc_free, 1)
                    elif kind == "adaG":
                        c0 = (g["j"] - 2 * D // 256) * 256
                        which = 0 if g["s"] == 0 else 1
                        nc.vector.tensor_copy(gate[:, which, c0:c0 + 256], src[:, 0:256]).then_inc(acc_free, 1)
                    elif kind == "wout":
                        s = 0 if g["tt"] >= TT_CTX else 1
                        if new(x_load, 16 * X_LOADS[g["l"]]):
                            dve.wait_ge(x_load, 16 * X_LOADS[g["l"]])
                        if new(acc_free, g["gates"]):
                            dve.wait_ge(acc_free, g["gates"])
                        if new(xr_done, g["xr"] - 1):
                            dve.wait_ge(xr_done, g["xr"] - 1)
                        c = slice(g["j"] * 256, (g["j"] + 1) * 256)
                        nc.vector.tensor_tensor(x_add[:, :], src[:, 0:256], gate[:, s, c], ALU.mult).then_inc(acc_free, 1)
                        if new(acc_free, g["v"]):
                            dve.wait_ge(acc_free, g["v"])
                        x = xres[:, g["tt"], c]
                        nc.vector.tensor_tensor(x, x, x_add[:, :], ALU.add).then_inc(xr_done, 1)
                elif ev == "L":
                    g = e["g"]
                    if new(h_done, g["high_n"]):
                        dve.wait_ge(h_done, g["high_n"])
                    if g["kind"] == "z":
                        o = o_t[:, g["t"], cols(g["tg"])]
                        ins = nc.vector.tensor_tensor(og_lo[:, g["t"], cols(g["tg"])], o, f(og_hi[:, g["t"], cols(g["tg"])]), ALU.subtract)
                    elif g["kind"] == "y":
                        c = cols(g["tg"])
                        ins = nc.vector.scalar_tensor_tensor(y_lo[:, g["t"], c], y2[:, g["t"], c], 0.5, f(y_hi[:, g["t"], c]), ALU.mult, ALU.subtract)
                    else:
                        ins = low_parts(*pieces(g))
                    ins.then_inc(l_done, 1)
                elif ev == "X":
                    u = e["u"]
                    r = u["n"] % 8
                    if new(s_done, u["n"] + 1):
                        dve.wait_ge(s_done, u["n"] + 1)
                    if u["n"] >= 8:
                        if new(exp_done, u["n"] - 7):
                            dve.wait_ge(exp_done, u["n"] - 7)
                    link(nc.vector.tensor_reduce(nmax[:, r:r + 1], wide[u["n"] % 2][:, u["lo"]:u["lo"] + u["width"]], AX.X, ALU.max, negate=True))
                    if u["branch"] == "swa":
                        scale = SCALE["swa"]
                    else:
                        i = 0 if u["branch"] == "mla" else u["h"]
                        scale = rq[:, i, u["tt"]:u["tt"] + 1]
                    nc.vector.tensor_scalar(nbias[:, r:r + 1], nmax[:, r:r + 1], scale, None, ALU.mult).then_inc(max_done, 1)
                elif ev == "N":
                    u = e["u"]
                    r = u["n"] % 8
                    if new(exp_done, u["n"] + 1):
                        dve.wait_ge(exp_done, u["n"] + 1)
                    link(nc.vector.reciprocal(einv[:, r:r + 1], esum[:, r:r + 1]))
                    nc.vector.tensor_scalar(e_of(u), e_of(u), einv[:, r:r + 1], None, ALU.mult).then_inc(norm_done, 1)
                elif ev == "T":
                    t = e["t"]
                    if new(pt_hi_ready, t["n"] + 1):
                        dve.wait_ge(pt_hi_ready, t["n"] + 1)
                    nc.vector.tensor_tensor(pt_of(t, 1), ptp[t["n"] % 2][:, 0:t["width"]], f(pt_of(t, 0)), ALU.subtract).then_inc(pt_lo_ready, 1)
                elif ev == "O":
                    pa = e["pa"]
                    own, _ = o_rows(pa)
                    if new(o_copied, pa["o"] + 1):
                        dve.wait_ge(o_copied, pa["o"] + 1)
                    k = len(pa["units"]) * P
                    nc.vector.tensor_tensor(o_t[own, pa["h"] // 2, o_tokens(pa)], acc[1][own, 0:k], o_half[own, 0:k], ALU.add).then_inc(o_free, 1)
                elif ev == "MOD":
                    if new(acc_free, e["free"]):
                        dve.wait_ge(acc_free, e["free"])
                    i = V_L + e["l"] * V_PER + V_NORM
                    for s in range(2):
                        ins = nc.vector.scalar_tensor_tensor(mod_a[:, s, :], mod_col[:, KD:2 * KD, s], 1.0, vec[:, i:i + KD], ALU.add, ALU.mult)
                    ins.then_inc(mod_ready, 1)
                elif ev == "AXT":
                    if new(tab_load, 32 * e["tab"]):
                        dve.wait_ge(tab_load, 32 * e["tab"])
                    i = V_L + e["l"] * V_PER + e["which"]
                    nc.vector.tensor_scalar(cos[:, :], cos[:, :], vec[:, i:i + 1], None, ALU.mult)
                    nc.vector.tensor_scalar(sin[:, :], sin[:, :], vec_sw[:, i:i + 1], None, ALU.mult).then_inc(axt_ready, 1)
                elif ev in ("XN", "FN"):
                    tt = e["tt"]
                    i = e["n"] + (LAYERS * TT if ev == "FN" else 0)
                    s = 0 if tt >= TT_CTX else 1
                    if new(x_stat, i + 1):
                        dve.wait_ge(x_stat, i + 1)
                    link(nc.vector.reciprocal(rstd[:, tt:tt + 1], rstd[:, tt:tt + 1]))
                    if ev == "FN":
                        if new(fin_load, 16):
                            dve.wait_ge(fin_load, 16)
                        nc.vector.scalar_tensor_tensor(xn[:, i % 2, :], xres[:, tt, :], rstd[:, tt:tt + 1], fin_w[:, :], ALU.mult, ALU.mult).then_inc(f_ready, 1)
                    else:
                        nc.vector.tensor_scalar(xn[:, i % 2, :], xres[:, tt, :], rstd[:, tt:tt + 1], None, ALU.mult).then_inc(x_n, 1)
                elif ev == "XM":
                    tt, i = e["tt"], e["n"]
                    s = 0 if tt >= TT_CTX else 1
                    if new(x_t, i + 1):
                        dve.wait_ge(x_t, i + 1)
                    if new(mod_ready, e["mod"]):
                        dve.wait_ge(mod_ready, e["mod"])
                    if i >= 2:
                        if new(x_l, i - 1):
                            dve.wait_ge(x_l, i - 1)
                    m = x_mod[:, i % 2, :].rearrange("p (k t) -> p k t", k=KD)
                    w = wide[i % 2][:, :].rearrange("p (k t) -> p k t", k=KD)
                    nc.vector.tensor_tensor(m, w, mod_a[:, s, :].unsqueeze(2).to_broadcast([P, KD, P]), ALU.mult).then_inc(x_f, 1)
                    if new(x_f, i + 1):
                        dve.wait_ge(x_f, i + 1)
                    nc.vector.tensor_tensor(m, m, mod_col[:, 0:KD, s].unsqueeze(2).to_broadcast([P, KD, P]), ALU.add).then_inc(x_b, 1)


def constants():
    import numpy as np
    pos = np.arange(SEQ)
    rows, colsp = (pos // GRID_W).astype(np.float32), (pos % GRID_W).astype(np.float32)

    def table(quarter):
        d = 2 * quarter
        freq = np.float32(THETA) ** (-np.arange(0, d, 2, dtype=np.float32) / np.float32(d))
        cs, sn = [], []
        for p in (rows, colsp):
            ang = (p[:, None] * freq[None, :]).astype(np.float32)
            cs += [np.cos(ang).T, np.cos(ang).T]
            sn += [-np.sin(ang).T, np.sin(ang).T]
        return np.concatenate(cs).astype(np.float32), np.concatenate(sn).astype(np.float32)

    c64, s64 = table(HD // 4)
    c32, s32 = table(MLA_ROPE // 4)
    out = {"cos_s": np.tile(c64, (2, 1)), "sin_s": np.tile(s64, (2, 1))}
    cm, sm = np.ones((P, SEQ), np.float32), np.zeros((P, SEQ), np.float32)
    cm[MLA_NOPE:MLA_K], sm[MLA_NOPE:MLA_K] = c32, s32
    out["cos_m"], out["sin_m"] = cm, sm
    k = np.zeros((P, K_END), np.float32)
    i, j = np.arange(P)[:, None], np.arange(P)[None, :]
    k[:, K_ID:K_ID + P] = i == j
    k[:, K_ONE:K_ONE + P] = 1.0
    k[:, K_BLK:K_BLK + P] = (i // HD) == (j // HD)
    k[:, K_MPREV:K_MPREV + P] = np.where(j >= i, 0.0, NEG)
    k[:, K_MNEXT:K_MNEXT + P] = np.where(j <= i, 0.0, NEG)
    k[[0, 2, 4], K_SEL] = 1.0
    k[[1, 3, 4], K_SEL + 1] = 1.0
    out["consts"] = k
    return out


INPUTS = ["x", "c", "ctx", "c_ctx", "ada_w", "ada_b", "norm_w", "w_in", "mla_q_norm", "mla_w_uq", "mla_kv_norm", "mla_w_ukv",
          "swa_sink", "ax_q_norm", "ax_k_norm", "w_o_mla", "w_o_swa", "w_o_ax", "w_out", "final_norm_w"]


def kernel(**inputs):
    import numpy as np
    import concourse.bacc as bacc
    from concourse.bass_utils import run_bass_kernel_spmd

    nc = bacc.Bacc("TRN2", target_bir_lowering=False, num_devices=1)
    arrays, t_in = {}, {}
    for name, a in list((k, inputs[k]) for k in INPUTS) + list(constants().items()):
        a = np.ascontiguousarray(a)
        arrays["in_" + name] = a
        t_in[name] = nc.dram_tensor("in_" + name, list(a.shape), mybir.dt.float32, kind="ExternalInput").ap()
    out = nc.dram_tensor("out_x", [1, SEQ, D], mybir.dt.float32, kind="ExternalOutput").ap()
    build(nc, t_in, out)
    r = run_bass_kernel_spmd(nc, [arrays], core_ids=[0])
    return r.results[0]["out_x"]
```
